# Optimizing a Trainium2 kernel written in Bass

```python
import functools
import jax, jax.numpy as jnp
from jax import lax
import numpy as np

D_MODEL = 1024
BATCH = 1
SEQ = 128
DEPTH = 2
DEC_BATCH = 1
DEC_SEQ = 1024
PAST_LEN = 256

GRID_W = 64
N_EVEN = (DEPTH + 1) // 2
N_ODD = DEPTH // 2
MOD_CHUNKS = 6
EPS = 1e-6
CONV_DIM = D_MODEL // 2
CONV_W = 3
N_Q_HEADS = 8
N_KV_HEADS = 2
GQA_GROUP = N_Q_HEADS // N_KV_HEADS
HEAD_DIM = (D_MODEL // 2) // N_Q_HEADS
WINDOW = 128
ATTN_BLOCK = 128
ROPE_BASE = 10000.0
AB_IN = 3 * CONV_DIM + (N_Q_HEADS + 2 * N_KV_HEADS) * HEAD_DIM
AB_OUT = CONV_DIM + N_Q_HEADS * HEAD_DIM
GLA_HEADS = 4
GLA_DK = (D_MODEL // 2) // GLA_HEADS
GLA_DV = D_MODEL // GLA_HEADS
GLA_RANK = 16
GLA_GATE_NORM = 16.0
GLA_CHUNK = 64
GLA_IN = 2 * GLA_HEADS * GLA_DK + 2 * GLA_HEADS * GLA_DV + 2 * GLA_RANK
D_FF = 4 * D_MODEL
NEG_INF = -1e30

kernel_name = 'hybrid_diffusion_conv_swa_gla_step'

def rms_norm(x, g):
    xf = x.astype(jnp.float32)
    y = xf * lax.rsqrt(jnp.mean(xf * xf, axis=-1, keepdims=True) + EPS)
    return (y * g.astype(jnp.float32)).astype(x.dtype)

def modulation(cond, w, b):
    m = jax.nn.silu(cond) @ w + b
    return [t[:, None, :] for t in jnp.split(m, MOD_CHUNKS, axis=-1)]

def sq_relu_mlp(h, w1, w2):
    return jnp.square(jax.nn.relu(h @ w1)) @ w2

def adaln_layer(x, cond, mod_w, mod_b, norm_g, w1, w2, mixer):
    sh1, sc1, gt1, sh2, sc2, gt2 = modulation(cond, mod_w, mod_b)
    h = rms_norm(x, norm_g[0]) * (1 + sc1) + sh1
    mix, aux = mixer(h)
    x = x + gt1 * rms_norm(mix, norm_g[1])
    h = rms_norm(x, norm_g[2]) * (1 + sc2) + sh2
    x = x + gt2 * rms_norm(sq_relu_mlp(h, w1, w2), norm_g[3])
    return x, aux

def short_conv(u, w):
    n = u.shape[1]
    pad = CONV_W // 2
    up = jnp.pad(u, ((0, 0), (pad, pad), (0, 0)))
    out = up[:, 0:n] * w[0]
    for i in range(1, CONV_W):
        out = out + up[:, i:i + n] * w[i]
    return out

def axial_rope(x):
    n = x.shape[1]
    rows = n // GRID_W
    pos_r = jnp.repeat(jnp.arange(rows), GRID_W)
    pos_c = jnp.tile(jnp.arange(GRID_W), rows)
    half = HEAD_DIM // 2
    quarter = half // 2
    inv = ROPE_BASE ** (-(jnp.arange(quarter, dtype=jnp.float32) * 2.0 / half))

    def rot(xa, pos):
        ang = pos.astype(jnp.float32)[:, None] * inv[None, :]
        cos = jnp.cos(ang)[None, :, None, :].astype(x.dtype)
        sin = jnp.sin(ang)[None, :, None, :].astype(x.dtype)
        x1, x2 = xa[..., :quarter], xa[..., quarter:]
        return jnp.concatenate([x1 * cos - x2 * sin, x2 * cos + x1 * sin], axis=-1)

    return jnp.concatenate([rot(x[..., :half], pos_r), rot(x[..., half:], pos_c)], axis=-1)

def sink_softmax(logits, sink):
    sb = jnp.broadcast_to(sink[:, :, None, None], logits.shape[:-1] + (1,))
    p = jax.nn.softmax(jnp.concatenate([logits, sb], axis=-1), axis=-1)
    return p[..., :-1]

def ctx_attention(q, k, v, sink):
    b, s = q.shape[:2]
    nb = s // ATTN_BLOCK
    scale = HEAD_DIM ** -0.5
    qb = q.reshape(b, nb, ATTN_BLOCK, N_KV_HEADS, GQA_GROUP, HEAD_DIM).swapaxes(0, 1)
    sink_f = sink.astype(jnp.float32).reshape(N_KV_HEADS, GQA_GROUP)

    def one_block(qblk):
        sc = jnp.einsum('bqhgd,bkhd->bhgqk', qblk, k, preferred_element_type=jnp.float32) * scale
        p = sink_softmax(sc, sink_f).astype(v.dtype)
        return jnp.einsum('bhgqk,bkhd->bqhgd', p, v)

    o = lax.map(one_block, qb)
    return o.swapaxes(0, 1).reshape(b, s, N_Q_HEADS * HEAD_DIM)

def latent_attention(q, k, v, k_ctx, v_ctx, sink):
    b, n = q.shape[:2]
    nb = n // ATTN_BLOCK
    scale = HEAD_DIM ** -0.5
    qb = q.reshape(b, nb, ATTN_BLOCK, N_KV_HEADS, GQA_GROUP, HEAD_DIM)

    def bands(t):
        tp = jnp.pad(t, ((0, 0), (ATTN_BLOCK, ATTN_BLOCK), (0, 0), (0, 0)))
        tp = tp.reshape(b, nb + 2, ATTN_BLOCK, N_KV_HEADS, HEAD_DIM)
        return jnp.concatenate([tp[:, :-2], tp[:, 1:-1], tp[:, 2:]], axis=2)

    kb, vb = bands(k), bands(v)
    blk = jnp.arange(nb)[:, None, None]
    qi = jnp.arange(ATTN_BLOCK)[None, :, None]
    kj = jnp.arange(3 * ATTN_BLOCK)[None, None, :]
    qpos = blk * ATTN_BLOCK + qi
    kpos = (blk - 1) * ATTN_BLOCK + kj
    valid = (jnp.abs(kpos - qpos) <= WINDOW) & (kpos >= 0) & (kpos < n)
    s_loc = jnp.einsum('bnqhgd,bnkhd->bnhgqk', qb, kb, preferred_element_type=jnp.float32) * scale
    s_loc = jnp.where(valid[None, :, None, None], s_loc, NEG_INF)
    s_ctx = jnp.einsum('bnqhgd,bphd->bnhgqp', qb, k_ctx, preferred_element_type=jnp.float32) * scale
    sink_f = sink.astype(jnp.float32).reshape(N_KV_HEADS, GQA_GROUP)
    p = sink_softmax(jnp.concatenate([s_loc, s_ctx], axis=-1), sink_f).astype(v.dtype)
    n_loc = 3 * ATTN_BLOCK
    o = (jnp.einsum('bnhgqk,bnkhd->bnqhgd', p[..., :n_loc], vb)
         + jnp.einsum('bnhgqp,bphd->bnqhgd', p[..., n_loc:], v_ctx))
    return o.reshape(b, n, N_Q_HEADS * HEAD_DIM)

def ab_split(h, w_in, conv_w):
    b, n, _ = h.shape
    z = h @ w_in
    c = CONV_DIM
    qd = N_Q_HEADS * HEAD_DIM
    kd = N_KV_HEADS * HEAD_DIM
    gate_b, gate_c, xin = z[..., :c], z[..., c:2 * c], z[..., 2 * c:3 * c]
    o = 3 * c
    q = z[..., o:o + qd].reshape(b, n, N_Q_HEADS, HEAD_DIM)
    k = z[..., o + qd:o + qd + kd].reshape(b, n, N_KV_HEADS, HEAD_DIM)
    v = z[..., o + qd + kd:].reshape(b, n, N_KV_HEADS, HEAD_DIM)
    conv_out = gate_b * short_conv(gate_c * xin, conv_w)
    return conv_out, q, k, v

def ab_context_mixer(h, w_in, conv_w, sink, w_out):
    conv_out, q, k, v = ab_split(h, w_in, conv_w)
    attn = ctx_attention(q, k, v, sink)
    return jnp.concatenate([conv_out, attn], axis=-1) @ w_out, (k, v)

def ab_latent_mixer(h, k_ctx, v_ctx, w_in, conv_w, sink, w_out):
    conv_out, q, k, v = ab_split(h, w_in, conv_w)
    attn = latent_attention(axial_rope(q), axial_rope(k), v, k_ctx.astype(v.dtype), v_ctx.astype(v.dtype), sink)
    return jnp.concatenate([conv_out, attn], axis=-1) @ w_out, None

def gla_split(h, w_in, gate_w, gate_b):
    b, n, _ = h.shape
    z = h @ w_in
    qk = GLA_HEADS * GLA_DK
    vd = GLA_HEADS * GLA_DV
    q = z[..., :qk]
    k = z[..., qk:2 * qk]
    v = z[..., 2 * qk:2 * qk + vd]
    og = z[..., 2 * qk + vd:2 * qk + 2 * vd]
    rf = z[..., 2 * qk + 2 * vd:2 * qk + 2 * vd + GLA_RANK]
    rb = z[..., 2 * qk + 2 * vd + GLA_RANK:]

    def heads(t, d):
        return t.reshape(b, n, GLA_HEADS, d).transpose(0, 2, 1, 3)

    def log_gate(r, i):
        return jax.nn.log_sigmoid((r @ gate_w[i] + gate_b[i]).astype(jnp.float32)) / GLA_GATE_NORM

    return (heads(q, GLA_DK) * GLA_DK ** -0.5, heads(k, GLA_DK), heads(v, GLA_DV), og,
            heads(log_gate(rf, 0), GLA_DK), heads(log_gate(rb, 1), GLA_DK))

def gla_chunk_scan(q, k, v, g, s0):
    b, hh, n, _ = q.shape
    nc = n // GLA_CHUNK

    def chunks(t):
        return t.astype(jnp.float32).reshape(b, hh, nc, GLA_CHUNK, t.shape[-1]).transpose(2, 0, 1, 3, 4)

    causal = jnp.tril(jnp.ones((GLA_CHUNK, GLA_CHUNK), dtype=bool))[:, :, None]

    def step(S, inp):
        qc, kc, vc, gc = inp
        bc = jnp.cumsum(gc, axis=2)
        o = jnp.einsum('bhcd,bhde->bhce', qc * jnp.exp(bc), S)
        diff = bc[:, :, :, None, :] - bc[:, :, None, :, :]
        decay = jnp.exp(jnp.where(causal, diff, -jnp.inf))
        att = jnp.einsum('bhid,bhijd->bhij', qc, decay * kc[:, :, None, :, :])
        o = o + jnp.einsum('bhij,bhje->bhie', att, vc)
        bl = bc[:, :, -1:, :]
        S = (jnp.exp(bl[:, :, 0, :])[..., None] * S
             + jnp.einsum('bhcd,bhce->bhde', kc * jnp.exp(bl - bc), vc))
        return S, o

    S, o = lax.scan(step, s0.astype(jnp.float32), (chunks(q), chunks(k), chunks(v), chunks(g)))
    return o.transpose(1, 2, 0, 3, 4).reshape(b, hh, n, GLA_DV), S

def gla_mixer(q, k, v, og, gf, gb, s0f, s0b, norm_g, w_out):
    b, _, n, _ = q.shape
    of, sf = gla_chunk_scan(q, k, v, gf, s0f)
    rev = lambda t: jnp.flip(t, axis=2)
    ob, sb = gla_chunk_scan(rev(q), rev(k), rev(v), rev(gb), s0b)
    o = (of + rev(ob)).transpose(0, 2, 1, 3)
    o = rms_norm(o, norm_g).reshape(b, n, GLA_HEADS * GLA_DV).astype(og.dtype) * jax.nn.silu(og)
    return o @ w_out, sf, sb

def gla_context_mixer(h, w_in, gate_w, gate_b, norm_g, w_out):
    q, k, v, og, gf, gb = gla_split(h, w_in, gate_w, gate_b)
    s0 = jnp.zeros((h.shape[0], GLA_HEADS, GLA_DK, GLA_DV), jnp.float32)
    out, sf, sb = gla_mixer(q, k, v, og, gf, gb, s0, s0, norm_g, w_out)
    return out, (sf, sb)

def gla_latent_mixer(h, s0f, s0b, w_in, gate_w, gate_b, norm_g, w_out):
    q, k, v, og, gf, gb = gla_split(h, w_in, gate_w, gate_b)
    out, _, _ = gla_mixer(q, k, v, og, gf, gb, s0f, s0b, norm_g, w_out)
    return out, None

def setup_inputs(seed: int = 0) -> dict:
    key = jax.random.key(seed)
    ks = jax.random.split(key, 24)
    f32 = jnp.float32

    def nrm(k, shape, s):
        return jax.random.normal(k, shape, f32) * s

    return {
        'x_prompt': nrm(ks[0], (BATCH, SEQ, D_MODEL), 1.0),
        'x_sample': nrm(ks[1], (DEC_BATCH, DEC_SEQ, D_MODEL), 1.0),
        'cache_k': nrm(ks[2], (DEC_BATCH, N_EVEN, PAST_LEN, N_KV_HEADS, HEAD_DIM), 1.0),
        'cache_v': nrm(ks[3], (DEC_BATCH, N_EVEN, PAST_LEN, N_KV_HEADS, HEAD_DIM), 1.0),
        'state_fwd': nrm(ks[4], (DEC_BATCH, N_ODD, GLA_HEADS, GLA_DK, GLA_DV), 0.5),
        'state_bwd': nrm(ks[5], (DEC_BATCH, N_ODD, GLA_HEADS, GLA_DK, GLA_DV), 0.5),
        'c': nrm(ks[6], (DEC_BATCH, D_MODEL), 1.0),
        'c_ctx': nrm(ks[7], (D_MODEL,), 1.0),
        'mod_w': nrm(ks[8], (DEPTH, D_MODEL, MOD_CHUNKS * D_MODEL), D_MODEL ** -0.5),
        'mod_b': nrm(ks[9], (DEPTH, MOD_CHUNKS * D_MODEL), 0.02),
        'norm_g': 1.0 + nrm(ks[10], (DEPTH, 4, D_MODEL), 0.05),
        'ab_w_in': nrm(ks[11], (N_EVEN, D_MODEL, AB_IN), D_MODEL ** -0.5),
        'conv_w': nrm(ks[12], (N_EVEN, CONV_W, CONV_DIM), CONV_W ** -0.5),
        'attn_sink': nrm(ks[13], (N_EVEN, N_Q_HEADS), 1.0),
        'ab_w_out': nrm(ks[14], (N_EVEN, AB_OUT, D_MODEL), AB_OUT ** -0.5),
        'gla_w_in': nrm(ks[15], (N_ODD, D_MODEL, GLA_IN), D_MODEL ** -0.5),
        'gla_gate_w': nrm(ks[16], (N_ODD, 2, GLA_RANK, GLA_HEADS * GLA_DK), GLA_RANK ** -0.5),
        'gla_gate_b': nrm(ks[17], (N_ODD, 2, GLA_HEADS * GLA_DK), 0.1),
        'gla_norm_g': 1.0 + nrm(ks[18], (N_ODD, GLA_DV), 0.05),
        'gla_w_out': nrm(ks[19], (N_ODD, GLA_HEADS * GLA_DV, D_MODEL), (GLA_HEADS * GLA_DV) ** -0.5),
        'mlp_w1': nrm(ks[20], (DEPTH, D_MODEL, D_FF), D_MODEL ** -0.5),
        'mlp_w2': nrm(ks[21], (DEPTH, D_FF, D_MODEL), D_FF ** -0.5),
    }

def reference(x_prompt, x_sample, cache_k, cache_v, state_fwd, state_bwd, c, c_ctx,
              mod_w, mod_b, norm_g, ab_w_in, conv_w, attn_sink, ab_w_out,
              gla_w_in, gla_gate_w, gla_gate_b, gla_norm_g, gla_w_out, mlp_w1, mlp_w2):
    x = x_prompt
    cond_ctx = c_ctx[None, :]
    ks, vs, sfs, sbs = [], [], [], []
    for l in range(DEPTH):
        j = l // 2
        if l % 2 == 0:
            mixer = functools.partial(ab_context_mixer, w_in=ab_w_in[j], conv_w=conv_w[j],
                                      sink=attn_sink[j], w_out=ab_w_out[j])
        else:
            mixer = functools.partial(gla_context_mixer, w_in=gla_w_in[j], gate_w=gla_gate_w[j],
                                      gate_b=gla_gate_b[j], norm_g=gla_norm_g[j], w_out=gla_w_out[j])
        x, aux = adaln_layer(x, cond_ctx, mod_w[l], mod_b[l], norm_g[l], mlp_w1[l], mlp_w2[l], mixer)
        if l % 2 == 0:
            ks.append(aux[0])
            vs.append(aux[1])
        else:
            sfs.append(aux[0])
            sbs.append(aux[1])
    y_prompt = x
    new_cache_k = jnp.stack(ks, axis=1)
    new_cache_v = jnp.stack(vs, axis=1)
    new_state_fwd = jnp.stack(sfs, axis=1)
    new_state_bwd = jnp.stack(sbs, axis=1)

    x = x_sample
    for l in range(DEPTH):
        j = l // 2
        if l % 2 == 0:
            mixer = functools.partial(ab_latent_mixer, k_ctx=cache_k[:, j], v_ctx=cache_v[:, j],
                                      w_in=ab_w_in[j], conv_w=conv_w[j], sink=attn_sink[j], w_out=ab_w_out[j])
        else:
            mixer = functools.partial(gla_latent_mixer, s0f=state_fwd[:, j], s0b=state_bwd[:, j],
                                      w_in=gla_w_in[j], gate_w=gla_gate_w[j], gate_b=gla_gate_b[j],
                                      norm_g=gla_norm_g[j], w_out=gla_w_out[j])
        x, _ = adaln_layer(x, c, mod_w[l], mod_b[l], norm_g[l], mlp_w1[l], mlp_w2[l], mixer)
    y_sample = x
    return (y_prompt, y_sample, new_cache_k, new_cache_v, new_state_fwd, new_state_bwd)


_drawn_inputs = setup_inputs


def setup_inputs(seed=0):
    import zlib

    import numpy as np

    out = dict(_drawn_inputs(seed))
    spreads = {}
    factors = {'cache_k': 3.552,
     'cache_v': 3.131,
     'state_fwd': 25.86,
     'state_bwd': 29.274,
     'attn_sink': 8.0,
     'gla_norm_g': 8.595}
    for name, (base, spread) in spreads.items():
        noise = np.random.default_rng([zlib.crc32(name.encode()), seed]).standard_normal(out[name].shape)
        drawn = base * np.exp(spread * noise) if base else spread * noise
        out[name] = __import__('jax').numpy.asarray(drawn.astype(out[name].dtype))
    for name, factor in factors.items():
        out[name] = (out[name] * factor).astype(out[name].dtype)
    return out
```

```python
from contextlib import ExitStack, contextmanager

import numpy as np
import concourse.bass as bass
from concourse import mybir

ALU = mybir.AluOpType
ACT = mybir.ActivationFunctionType
F32 = mybir.dt.float32
F32R = mybir.dt.float32r
U8 = mybir.dt.uint8
AX_X = mybir.AxisListType.X

P = 128
D = 1024
DC = D // P
TILES = 9
TOK = TILES * P
GROUPS = 3
GT = TILES // GROUPS
GN = GT * P
LAT = TOK - P
EPS = 1e-6
KINDS = 6
CONV = D // 2
CC = CONV // P
HD = 64
PAST = 256
FF = 4 * D
PAIRS = FF // P // 2
AB_IN = 2304
GH = 4
DV = 256
RANK = 16
GLA_IN = 3104
GATE_NORM = 16.0
LEVELS = [64, 32, 16, 8, 4, 2, 1]
SLOTS = 4
BAND = 1e30
STAGE = 99


class Tally:

    def __init__(self, start=()):
        self.n = dict(start)
        self.i = None
        self.per = {}

    def last(self, sem, lag=0):
        v = self.n.get(sem.name, 0) - lag
        if self.i is not None and self.per.get(sem.name, 0):
            v = self.i * self.per[sem.name] + v
        return v

    def next(self, sem, n=1):
        self.n[sem.name] = self.n.get(sem.name, 0) + n
        return self.last(sem)

    add = next

    @contextmanager
    def loop(self, eng, times, per):
        per = {s.name: n for s, n in per}
        before = dict(self.n)
        with eng.Fori(0, times) as i:
            self.i, self.per = i, per
            yield i
            self.i, self.per = None, {}
        for name in set(self.n) | set(per):
            grown = self.n.get(name, 0) - before.get(name, 0)
            assert grown == per.get(name, 0), (name, grown, per.get(name, 0))
            self.n[name] = before.get(name, 0) + grown * times


def build(nc, io):
    base = 16512
    Q = TILES * D * 4
    RA, RB, RC, RD = (base + i * Q for i in range(4))
    RW = base + 4 * Q
    PANEL = D * 4
    RS = RW + 3 * SLOTS * PANEL
    RK = RS + 9248

    def at(name, shape, dt, offset):
        return nc.alloc_sbuf_tensor_at(name, shape, dt, offset=offset)

    x_in = at("x_in", [P, TILES, D], F32, RB)
    mod_w = [at(f"mod_w{i}", [P, KINDS * D], F32, r) for i, r in enumerate((RA, RC))]
    xb = [at("xb0", [P, GT, DC, P], F32, RD), at("xb1", [P, GT, DC, P], F32, RD + 24576)]
    sq = at("sq", [P, GT, DC, P], F32, RD + 12288)

    def acts(name, dt, r, chunks=DC):
        return at(name, [P, TILES, chunks, P], dt, r)

    h_ac = (acts("h_hi_a", F32R, RA), acts("h_lo_c", F32R, RC))
    h_bc = (acts("h_hi_b", F32R, RB), acts("h_lo_c2", F32R, RC))
    t_b = acts("t_b", F32, RB)
    t_a = acts("t_a", F32, RA)
    hidden = [[at(f"hid{p}{x}", [P, 2, TOK], F32R, RD + 18432 * p + 9216 * x) for x in range(2)] for p in range(2)]
    conv_hi = acts("conv_hi", F32R, RD, CC)
    conv_lo = acts("conv_lo", F32R, RD + Q // 2, CC)
    at_hi = acts("at_hi", F32R, RC, CC)
    at_lo = acts("at_lo", F32R, RC + Q // 2, CC)
    m_hi = acts("m_hi", F32R, RC)
    m_lo = acts("m_lo", F32R, RB)
    q_t = at("q_t", [P, 4, TOK], F32, RB)
    k_t = at("k_t", [P, TOK], F32, RB + 18432)
    v_t = at("v_t", [P, TOK], F32, RB + 23040)
    y_cv = at("y_cv", [P, 1154], F32, RB + 27648)
    m_f = [at(f"m_f{i}", [P, GN], F32, RB + 32288 + 1536 * i) for i in range(2)]
    cw = at("cw", [P, 3], F32, RB + 35392)
    c_cv = at("c_cv", [P, TOK], F32, RS)
    u_cv = at("u_cv", [P, 1156], F32, RS + 4608)
    o = RA
    cosT = at("cosT", [P, LAT], F32, o)
    sinT = at("sinT", [P, LAT], F32, o + 4096)
    v_n = at("v_n", [P, TILES, P], F32, o + 8192)
    kc_n = at("kc_n", [P, 2, P], F32, o + 12800)
    v_c = at("v_c", [P, 2, P], F32, o + 13824)
    kc_t = at("kc_t", [P, 2 * P], F32, o + 14848)
    k_out = at("k_out", [P, P], F32, o + 15872)
    rot = at("rot", [P, P], F32, o + 16384)
    band = at("band", [P, 2, P], F32, o + 16896)
    rt1 = at("rt1", [P, 512], F32, o + 17920)
    rt2 = at("rt2", [P, 512], F32, o + 19968)
    prob = [at(f"prob{i}", [P, 640], F32, o + 22016 + 2560 * i) for i in range(2)]
    prT = [at(f"prT{i}", [P, 5, P], F32, o + 27136 + 2560 * i) for i in range(2)]
    smx = at("smx", [P, 2, 8], F32, o + 32256)
    gq = at("gq", [P, TILES, GH, P], F32, RD)
    gk = at("gk", [P, TILES, GH, P], F32, RD + Q // 2)
    gv = at("gv", [P, TILES, D], F32, RB)
    bc_f = at("bc_f", [P, TILES, GH, P], F32, RA)
    bc_b = at("bc_b", [P, TILES, GH, P], F32, RA + Q // 2)
    o_b = at("o_b", [P, TILES, D], F32, RC)
    v_tmp = [at(f"v_tmp{i}", [P, GN], F32, RS + 1536 * i) for i in range(2)]
    og_s = [at(f"og_s{i}", [P, GN], F32, RS + (0, 1536, 7680)[i]) for i in range(3)]
    r_t = at("r_t", [32, TOK], F32, RS + 3072)
    relu = [at(f"relu{i}", [P, GN], F32, RS + 1536 * i) for i in range(2)]
    sqr = [at(f"sqr{i}", [P, GN], F32, RS + 3072 + 1536 * i) for i in range(2)]
    raw = at("raw", [P, SLOTS, DC, P], F32, RW)
    w_hi = at("w_hi", [P, SLOTS, DC, P], F32R, RW + SLOTS * PANEL)
    w_lo = at("w_lo", [P, SLOTS, DC, P], F32R, RW + 2 * SLOTS * PANEL)
    w = RW
    st = at("st", [P, GH, DV], F32, w)
    dd = [at(f"dd{i}", [P, GH, P], F32, w + 4096 + 2048 * i) for i in range(2)]
    ee = [at(f"ee{i}", [P, GH, P], F32, w + 8192 + 2048 * i) for i in range(2)]
    xx = [at(f"xx{i}", [P, GH, P], F32, w + 12288 + 2048 * i) for i in range(2)]
    qh = at("qh", [P, GH, P], F32, w + 16384)
    kh = at("kh", [P, GH, P], F32, w + 18432)
    khn = at("khn", [P, GH, P], F32, w + 20480)
    att = [at(f"att{i}", [P, GH, P], F32, w + 22528 + 2048 * i) for i in range(2)]
    oo = at("oo", [P, D], F32, w + 26624)
    og = [at(f"og{i}", [P, DC, P], F32, w + 30720 + 4096 * i) for i in range(2)]
    mm_ = at("mm_", [P, DC, P], F32, w + 38912)
    masks = at("masks", [P, 2 * len(LEVELS), P], F32, RS)
    tot_b = at("tot_b", [P, TILES, GH], F32, w + 44800)
    dec = at("dec", [P, 2 * TILES, GH], F32, w + 44960)
    rs4 = at("rs4", [P, 2, GH], F32, w + 45248)
    junk = at("junk", [P, DV], F32, w + 45280)
    gw = at("gw", [32, 2, GH * P], F32, w + 26624)
    g_x = [at(f"g_x{i}", [P, GN], F32, w + 30720 + 1536 * i) for i in range(2)]
    g_l = [at(f"g_l{i}", [P, GN], F32, w + 33792 + 1536 * i) for i in range(2)]
    g_g = [at(f"g_g{i}", [P, GN], F32, w + 36864 + 1536 * i) for i in range(2)]
    k = RK
    ident = at("ident", [P, P], F32, k)
    ones = at("ones", [P, P], F32, k + 512)
    vec1 = at("vec1", [P, P], F32, k + 1024)
    vec2 = at("vec2", [P, P], F32, k + 1536)
    mods = at("mods", [P, 2, KINDS, DC, 2], F32, k + 2048)
    csil = at("csil", [P, DC, 2], F32, k + 2816)
    sink = at("sink", [P, 8], F32, k + 2880)
    eps = at("eps", [P, 1], F32, k + 2912)
    one1 = at("one1", [P, 1], F32, k + 2944)
    ss = at("ss", [P, GN], F32, k + 2976)
    rt = at("rt", [P, GN], F32, k + 4512)
    assert k + 6048 <= nc.sbuf_usable_end
    y_sb = at("y_sb", [P, TILES, D], F32, RB)
    rows1 = at("rows1", [P, P], F32, RS)
    rows2 = at("rows2", [P, P], F32, RS + 512)

    x_d = io["x_scratch"]
    og_d = io["og_scratch"]

    with ExitStack() as ctx:
        ps = ctx.enter_context(nc.psum_tensor("ps", [P, 8, 512], F32))
        psf = ps[:, :, :].rearrange("p b n -> p (b n)")

        def sem(name):
            return ctx.enter_context(nc.semaphore(name))

        const_in = sem("const_in")
        xin_in = sem("xin_in")
        mod_landed = [sem(f"mod_landed{i}") for i in range(2)]
        raw_landed = [sem(f"raw_landed{i}") for i in range(SLOTS)]
        hi_split = sem("hi_split")
        panel_split = sem("panel_split")
        panel_used = sem("panel_used")
        unit_ready = [sem(f"unit_ready{i}") for i in range(3)]
        unit_free = [sem(f"unit_free{i}") for i in range(3)]
        acc_ready = [sem(f"acc_ready{i}") for i in range(4)]
        acc_free = [sem(f"acc_free{i}") for i in range(4)]
        dve_set = sem("dve_set")
        dve_own = sem("dve_own")
        act_own = sem("act_own")
        vec_turned = sem("vec_turned")
        vec_copied = sem("vec_copied")
        csil_ready = sem("csil_ready")
        mods_ready = sem("mods_ready")
        n_sq = sem("n_sq")
        n_ss = sem("n_ss")
        n_sum = sem("n_sum")
        n_rt = sem("n_rt")
        n_x = sem("n_x")
        n_xn = sem("n_xn")
        n_h = sem("n_h")
        n_hi = sem("n_hi")
        n_lo = sem("n_lo")
        x_stored = sem("x_stored")
        x_loaded = [sem(f"x_loaded{i}") for i in range(2)]
        t_zero = sem("t_zero")
        sq_done = sem("sq_done")
        hid_hi = sem("hid_hi")
        hid_lo = sem("hid_lo")
        u_clear = sem("u_clear")
        conv_u = sem("conv_u")
        conv_y = sem("conv_y")
        conv_m = sem("conv_m")
        att_in = sem("att_in")
        rope_done = sem("rope_done")
        kv_turned = sem("kv_turned")
        s_ready = sem("s_ready")
        s_max = sem("s_max")
        s_exp = sem("s_exp")
        s_norm = sem("s_norm")
        pt_ready = sem("pt_ready")
        pt_a = sem("pt_a")
        pt_v = sem("pt_v")
        pv_ready = sem("pv_ready")
        ao_hi = sem("ao_hi")
        ao_lo = sem("ao_lo")
        cache_out = sem("cache_out")
        y_out = sem("y_out")
        og_out = [sem(f"og_out{i}") for i in range(3)]
        act_gate = sem("act_gate")
        sp_gate = sem("sp_gate")
        og_in = [sem(f"og_in{i}") for i in range(2)]
        gla_in = sem("gla_in")
        mask_in = sem("mask_in")
        v_tmp_ready = sem("v_tmp_ready")
        g_ln = sem("g_ln")
        g_sum = sem("g_sum")
        d_ready = sem("d_ready")
        e_ready = sem("e_ready")
        xt_ready = sem("xt_ready")
        gram_ready = sem("gram_ready")
        gram_taken = sem("gram_taken")
        diag_ready = sem("diag_ready")
        khn_t = sem("khn_t")
        khn_ready = sem("khn_ready")
        ob_ready = sem("ob_ready")
        ob_taken = sem("ob_taken")
        upd_ready = sem("upd_ready")
        st_ready = sem("st_ready")
        st_in = sem("st_in")
        st_out = sem("st_out")
        o_ready = sem("o_ready")
        o_sum = sem("o_sum")
        o_sq = sem("o_sq")
        o_nrm = sem("o_nrm")
        ot_ready = sem("ot_ready")
        ot_taken = sem("ot_taken")
        gm_hi = sem("gm_hi")
        gm_lo = sem("gm_lo")
        dec_ready = sem("dec_ready")
        gla_free = sem("gla_free")

        block = ctx.enter_context(nc.Block())

        N_CONST = 12
        X_TILES = TILES

        def attention_steps():
            out = []
            for b in range(TILES):
                if b == 0:
                    tiles = [("own", 0)]
                else:
                    tiles = [("ctx", 0), ("ctx", 1)] + [("own", t) for t in (b - 1, b, b + 1) if 1 <= t < TILES]
                out += [(b, j, u, tiles) for j in range(4) for u in range(2)]
            return out

        def s_bank(step):
            return psf[:, (3 + 2 * (step % 2)) * 512:(5 + 2 * (step % 2)) * 512]

        def o_bank(step):
            return (2, 7)[(step // 2) % 2]

        @block.sync
        def _(sp):
            T = Tally()

            def small(dst, src):
                sp.dma_start(dst, src).then_inc(const_in, 16)

            small(ident[:], io["c_ident"])
            small(rows1[0:96, :], io["mod_b"].rearrange("l (r n) -> (l r) n", n=P))
            small(rows1[96:104, :], io["c_ctx"].rearrange("(r n) -> r n", n=P))
            small(rows1[104:112, :], io["c"].rearrange("b (r n) -> (b r) n", n=P))
            small(rows1[112:124, :], io["conv_w"].rearrange("a w (r n) -> (a w r) n", n=P))
            small(rows2[0:64, :], io["norm_g"].rearrange("l i (r n) -> (l i r) n", n=P))
            small(rows2[64:72, :], io["gla_gate_b"].rearrange("a d (r n) -> (a d r) n", n=P))
            small(rows2[72:74, :], io["gla_norm_g"].rearrange("a (r n) -> (a r) n", n=P))
            small(sink[:], io["attn_sink"].partition_broadcast(P).rearrange("p a h -> p (a h)"))
            small(x_in[:, 0, :], io["x_prompt"][0])
            small(x_in[:, 1:5, :], io["x_sample"][0, 0:512].rearrange("(t p) d -> p t d", p=P))
            small(x_in[:, 5:9, :], io["x_sample"][0, 512:1024].rearrange("(t p) d -> p t d", p=P))

            for layer in range(2):
                rows = io["mod_w"][layer].rearrange("(i b p) n -> i b p n", b=2, p=P)
                with T.loop(sp, DC // 2, [(acc_free[0], 1), (acc_free[1], 1)]) as i:
                    for b in range(2):
                        sp.wait_ge(acc_free[b], T.next(acc_free[b]))
                        sp.sem_inc(sp_gate, 1)
                        sp.dma_start(mod_w[b][:], rows[i, b]).then_inc(mod_landed[b], 16)

            def panel(slot, pieces):
                sp.wait_ge(panel_split, T.next(panel_split))
                sp.sem_inc(sp_gate, 1)
                for dst, src in pieces:
                    sp.dma_start(dst, src).then_inc(raw_landed[slot], 16)

            def columns(w, f):
                return w.rearrange("(k p) (f n) -> f p k n", p=P, n=P)[f]

            w_in = io["ab_w_in"][0]
            with T.loop(sp, CC, [(panel_split, 3)]) as i:
                for s, part in enumerate((1, 2, 0)):
                    src = w_in[:, part * CONV:(part + 1) * CONV]
                    panel(s, [(raw[:, s], columns(src, i))])
            kv = w_in[:, 4 * CONV:4 * CONV + 2 * P]
            for s in range(2):
                panel(s, [(raw[:, s], columns(kv, s))])
            qw = w_in[:, 3 * CONV:4 * CONV].rearrange("(k p) (u j n) -> u j p k n", p=P, u=2, n=HD)
            for j in range(4):
                s = (2 + j) % 3
                panel(s, [(raw[:, s, :, 0:HD], qw[0, j]), (raw[:, s, :, HD:P], qw[1, j])])

            def out_panel(slot, f):
                w_out = io["ab_w_out"][0]
                cols = w_out[0:CONV, :].rearrange("(k p) (f n) -> f p k n", p=P, n=P)
                lo = w_out[CONV:CONV + 4 * HD, :].rearrange("(j p) (f n) -> f p j n", p=HD, n=P)
                hi = w_out[CONV + 4 * HD:, :].rearrange("(j p) (f n) -> f p j n", p=HD, n=P)
                panel(slot, [(raw[:, slot, 0:CC], cols[f]), (raw[0:HD, slot, CC:DC], lo[f]),
                             (raw[HD:P, slot, CC:DC], hi[f])])

            with T.loop(sp, 2, [(panel_split, 4)]) as i:
                for s in range(SLOTS):
                    out_panel(s, i * 4 + s)

            def mlp_panels(layer, s0):
                w1, w2 = io["mlp_w1"][layer], io["mlp_w2"][layer]
                rows = w2.rearrange("(f p) (k n) -> f p k n", p=P, n=P)
                for s in range(2):
                    panel((s0 + s) % SLOTS, [(raw[:, (s0 + s) % SLOTS], columns(w1, s))])
                with T.loop(sp, PAIRS - 1, [(panel_split, 4)]) as i:
                    for s in range(2):
                        slot = (s0 + 2 + s) % SLOTS
                        panel(slot, [(raw[:, slot], columns(w1, i * 2 + 2 + s))])
                    for s in range(2):
                        slot = (s0 + s) % SLOTS
                        panel(slot, [(raw[:, slot], rows[i * 2 + s])])
                for s in range(2):
                    slot = (s0 + 2 + s) % SLOTS
                    panel(slot, [(raw[:, slot], rows[2 * PAIRS - 2 + s])])

            mlp_panels(0, 0)
            if STAGE < 2:
                return
            gla = io["gla_w_in"][0]
            panel(0, [(raw[:, 0, :, 0:2 * RANK], gla[:, GLA_IN - 2 * RANK:].rearrange("(k p) n -> p k n", p=P))])
            for part in range(2):
                with T.loop(sp, 3, [(panel_split, 4)]) as i:
                    for s in range(4):
                        src = gla[:, 0:3 * D]
                        panel((1 + s) % SLOTS, [(raw[:, (1 + s) % SLOTS], columns(src, i * 4 + s + 12 * part))])
            sp.wait_ge(gla_free, 1)
            with T.loop(sp, 2, [(panel_split, 4)]) as i:
                for s in range(4):
                    panel((1 + s) % SLOTS, [(raw[:, (1 + s) % SLOTS], columns(io["gla_w_out"][0], i * 4 + s))])
            mlp_panels(1, 1)

        def terms():
            out = []
            for tile in [0] + list(range(TILES - 1, 0, -1)):
                if tile != 1:
                    out.append(("k", 1, tile, None))
                if tile:
                    out.append(("q", 1, tile, None))
            for tile in range(TILES):
                for level in range(len(LEVELS)):
                    out += [("pair", 0, tile, level), ("pair", 1, tile, level)]
                if tile:
                    out.append(("q", 0, tile, None))
                if tile < TILES - 1:
                    out.append(("k", 0, tile, None))
            return out

        def relative(kind, d):
            return kind == "pair" or (kind, d) in (("k", 0), ("q", 1))

        def halves(t, level):
            return t.rearrange("p h (b s n) -> p (h b) s n", s=2, n=LEVELS[level])

        def pool_gla(pool, T):
            pool.wait_ge(g_sum, 24)
            used = []
            for i, (kind, d, tile, level) in enumerate(terms()):
                if not relative(kind, d):
                    continue
                n = len(used)
                if len(used) >= 2:
                    pool.wait_ge(e_ready, used[-2] + 1)
                b = bc_b if d else bc_f
                if kind == "pair":
                    nn = LEVELS[level]
                    v = b[:, tile].rearrange("p h (b m) -> p (h b) m", m=2 * nn)
                    ref = v[:, :, nn:nn + 1] if d else v[:, :, nn - 1:nn]
                    out = dd[n % 2][:, :, :].rearrange("p h (b m) -> p (h b) m", m=2 * nn)
                    nc.gpsimd.tensor_tensor(out, v, ref.broadcast_to(v.shape), ALU.subtract).then_inc(d_ready, 1)
                else:
                    ref = tot_b[:, tile].unsqueeze(2) if d else b[:, tile, :, P - 1:P]
                    nc.gpsimd.tensor_tensor(dd[n % 2][:], b[:, tile], ref.broadcast_to([P, GH, P]),
                                            ALU.subtract).then_inc(d_ready, 1)
                used.append(i)

        @block.gpsimd
        def _(pool):
            T = Tally()
            nc.gpsimd.memset(one1[:], 1.0).then_inc(hi_split, 1)
            pool.wait_ge(hi_split, T.next(hi_split))
            pool.sem_inc(panel_split, 3)

            def split(slot, pieces=1, width=P):
                pool.wait_ge(raw_landed[slot], T.next(raw_landed[slot], 16 * pieces))
                pool.wait_ge(panel_used, T.next(panel_used))
                nc.gpsimd.tensor_tensor(w_hi[:, slot, :, 0:width], raw[:, slot, :, 0:width],
                                        one1[:].unsqueeze(1).broadcast_to([P, DC, width]), ALU.mult).then_inc(hi_split, 1)
                pool.wait_ge(hi_split, T.next(hi_split))
                nc.gpsimd.tensor_tensor(w_lo[:, slot, :, 0:width], raw[:, slot, :, 0:width],
                                        w_hi[:, slot, :, 0:width].bitcast(F32), ALU.subtract).then_inc(panel_split, 1)

            def per(*slots, pieces=1):
                return ([(raw_landed[s], 16 * pieces * slots.count(s)) for s in sorted(set(slots))]
                        + [(panel_used, len(slots)), (hi_split, len(slots))])

            with T.loop(pool, CC, per(0, 1, 2)):
                for s in range(3):
                    split(s)
            for s in range(2):
                split(s)
            for j in range(4):
                split((2 + j) % 3, pieces=2)
            with T.loop(pool, 2, per(0, 1, 2, 3, pieces=3)):
                for s in range(4):
                    split(s, pieces=3)

            def mlp_splits(s0):
                for s in range(2):
                    split((s0 + s) % SLOTS)
                with T.loop(pool, PAIRS - 1, per(0, 1, 2, 3)):
                    for s in (2, 3, 0, 1):
                        split((s0 + s) % SLOTS)
                for s in (2, 3):
                    split((s0 + s) % SLOTS)

            mlp_splits(0)
            if STAGE < 2:
                return
            split(0, width=2 * RANK)
            for part in range(2):
                with T.loop(pool, 3, per(0, 1, 2, 3)):
                    for s in range(4):
                        split((1 + s) % SLOTS)
            pool_gla(pool, T)
            with T.loop(pool, 2, per(0, 1, 2, 3)):
                for s in range(4):
                    split((1 + s) % SLOTS)
            mlp_splits(1)

        @block.scalar
        def _(act):
            T = Tally()
            for b in range(3):
                act.sem_inc(unit_free[b], 1)
                T.add(unit_free[b])

            def take(out, bank, func=ACT.Copy, **kw):
                act.wait_ge(unit_ready[bank], T.next(unit_ready[bank]))
                nc.scalar.activation(out, ps[:, bank, 0:GN] if len(out.shape) == 2 else
                                     ps[:, bank, 0:GN].rearrange("p (t n) -> p t n", t=out.shape[1]),
                                     func, **kw).then_inc(unit_free[bank], 1)
                T.add(unit_free[bank])

            def own(ins):
                ins.then_inc(act_own, 1)
                act.wait_ge(act_own, T.next(act_own))

            act.wait_ge(vec_copied, 1)
            nc.scalar.activation(csil[:, :, :], vec1[:, 96:112].rearrange("p (c k) -> p k c", c=2),
                                 ACT.Silu).then_inc(csil_ready, 1)

            def root():
                act.wait_ge(n_sum, T.next(n_sum))
                nc.scalar.activation(rt[:], ps[:, 7, 0:GN], ACT.Sqrt, bias=eps[:, 0:1], scale=1.0 / D).then_inc(n_rt, 1)
                T.add(n_rt)

            def affine(n, layer, kind):
                def go(src, dst, hi):
                    act.wait_ge(n_xn, T.next(n_xn))
                    for c in range(DC):
                        for lo, up, cond in ([(0, 1, 0), (1, 3, 1)] if n == 0 else [(0, 3, 1)]):
                            last = nc.scalar.activation(dst[:, lo:up, c, :], src[:, lo:up, c, :], ACT.Identity,
                                                        bias=mods[:, layer, kind, c, cond:cond + 1],
                                                        scale=mods[:, layer, kind + 1, c, cond:cond + 1])
                    last.then_inc(n_h, 1)
                    act.wait_ge(n_h, T.next(n_h))
                    nc.scalar.activation(hi[:, 3 * n:3 * n + 3], dst[:], ACT.Copy).then_inc(n_hi, 1)
                    T.add(n_hi)
                return go

            def store_x(n):
                act.dma_start(x_d[3 * n:3 * n + 3].rearrange("t p m -> p t m"),
                              xb[n % 2][:].rearrange("p t c n -> p t (c n)")).then_inc(x_stored, 16)
                T.add(x_stored, 16)

            def load_x(n):
                act.dma_start(xb[n % 2][:].rearrange("p t c n -> p t (c n)"),
                              x_d[3 * n:3 * n + 3].rearrange("t p m -> p t m")).then_inc(x_loaded[n % 2], 16)

            for n in range(GROUPS):
                if n == 2:
                    act.wait_ge(x_stored, T.last(x_stored))
                    act.wait_ge(n_xn, T.last(n_xn))
                for c in range(DC):
                    take(xb[n % 2][:, :, c, :], (n * DC + c) % 3)
                for b in range(3):
                    act.wait_ge(unit_free[b], T.last(unit_free[b]))
                if n:
                    act.wait_ge(n_lo, n)
                store_x(n)
                nc.scalar.activation(sq[:], xb[n % 2][:], ACT.Square).then_inc(n_sq, 1)
                T.add(n_sq)
                root()
                act.wait_ge(mods_ready, 1)
                affine(n, 0, 0)(t_b[:, 3 * n:3 * n + 3], sq, h_ac[0])
            T.n[n_lo.name] = GROUPS


            def both_norms(t, hi, layer, kind, final=False):
                act.wait_ge(x_stored, T.last(x_stored))
                for n in range(2):
                    load_x(n)
                for n in range(GROUPS):
                    if n and not final:
                        act.wait_ge(n_lo, T.next(n_lo))
                    elif n:
                        act.wait_ge(n_x, T.last(n_x))
                    nc.scalar.activation(sq[:], t[:, 3 * n:3 * n + 3], ACT.Square).then_inc(n_sq, 1)
                    T.add(n_sq)
                    root()
                    act.wait_ge(n_x, T.next(n_x))
                    if not final:
                        store_x(n)
                        nc.scalar.activation(sq[:], xb[n % 2][:], ACT.Square).then_inc(n_sq, 1)
                        T.add(n_sq)
                        root()
                        affine(n, layer, kind)(t[:, 3 * n:3 * n + 3], sq, hi)
                        if n == 0:
                            act.wait_ge(x_stored, T.last(x_stored))
                            load_x(2)
                    else:
                        for c in range(DC):
                            take(y_sb[:, 3 * n:3 * n + 3, c * P:(c + 1) * P], (n * DC + c) % 3)
                        for b in range(3):
                            act.wait_ge(unit_free[b], T.last(unit_free[b]))
                        if n == 0:
                            load_x(2)
                            act.dma_start(io["y_prompt"][0], y_sb[:, 0, :]).then_inc(y_out, 16)
                            act.dma_start(io["y_sample"][0, 0:256].rearrange("(t p) d -> p t d", p=P),
                                          y_sb[:, 1:3, :]).then_inc(y_out, 16)
                        else:
                            act.dma_start(io["y_sample"][0, GN * n - P:GN * (n + 1) - P].rearrange("(t p) d -> p t d", p=P),
                                          y_sb[:, 3 * n:3 * n + 3, :]).then_inc(y_out, 16)
                if not final:
                    T.add(n_lo)

            per = [(unit_ready[b], 3) for b in range(3)] + [(unit_free[b], 3) for b in range(3)]
            with T.loop(act, CC, per + [(conv_m, 3), (conv_y, 1), (conv_u, 3)]):
                for n in range(GROUPS):
                    act.wait_ge(conv_m, T.next(conv_m))
                    take(c_cv[:, GN * n:GN * (n + 1)], n)
                act.wait_ge(conv_y, T.next(conv_y))
                act.wait_ge(u_clear, 1)
                for n in range(GROUPS):
                    act.wait_ge(unit_ready[n], T.next(unit_ready[n]))
                    if n == 0:
                        nc.scalar.activation(u_cv[:, 1:P + 1], ps[:, n, 0:P], ACT.Copy)
                        nc.scalar.activation(u_cv[:, P + 3:GN + 3], ps[:, n, P:GN], ACT.Copy).then_inc(unit_free[n], 1)
                    else:
                        nc.scalar.activation(u_cv[:, GN * n + 3:GN * (n + 1) + 3], ps[:, n, 0:GN],
                                             ACT.Copy).then_inc(unit_free[n], 1)
                    T.add(unit_free[n])
                for n in range(GROUPS):
                    act.wait_ge(conv_u, T.next(conv_u))
                    take(c_cv[:, GN * n:GN * (n + 1)], n)
            for dst, scale in [(k_t[:], 1.0), (v_t[:], 1.0)] + [(q_t[:, j, :], HD ** -0.5) for j in range(4)]:
                for n in range(GROUPS):
                    take(dst[:, GN * n:GN * (n + 1)], n, scale=scale)

            for b in range(3):
                act.wait_ge(unit_free[b], T.last(unit_free[b]))
            for dst, src in ((cosT[:], io["c_cos"]), (sinT[:], io["c_sin"]), (rot[:], io["c_rot"]), (band[:], io["c_band"]),
                             (kc_n[:], io["cache_k"][0, 0].rearrange("(t p) h d -> p t (h d)", p=P)),
                             (v_c[:], io["cache_v"][0, 0].rearrange("(t p) h d -> p t (h d)", p=P))):
                act.dma_start(dst, src).then_inc(att_in, 16)
            for n in range(GROUPS):
                take(v_n[:, 3 * n:3 * n + 3, :], n)
            act.wait_ge(unit_ready[0], T.next(unit_ready[0]))
            nc.scalar.activation(kc_t[:], ps[:, 0, 0:2 * P], ACT.Copy)
            nc.scalar.activation(k_out[:], ps[:, 0, 2 * P:3 * P], ACT.Copy).then_inc(unit_free[0], 1)
            T.add(unit_free[0])
            for b in range(3):
                act.wait_ge(unit_free[b], T.last(unit_free[b]))
            act.dma_start(io["new_cache_k"][0, 0].rearrange("s h d -> s (h d)"), k_out[:]).then_inc(cache_out, 16)
            act.dma_start(io["new_cache_v"][0, 0].rearrange("s h d -> s (h d)"), v_n[:, 0, :]).then_inc(cache_out, 16)

            steps = attention_steps()
            for it in range(len(steps) + 3):
                if 2 <= it < len(steps) + 2:
                    b, j, u, tiles = steps[it - 2]
                    act.wait_ge(pt_ready, it - 1)
                    if it >= 4:
                        act.wait_ge(pv_ready, it - 3)
                    m = min(3, len(tiles))
                    nc.scalar.activation(prT[it % 2][:, 0:m, :], ps[:, 0, 0:m * P].rearrange("p (t n) -> p t n", t=m),
                                         ACT.Copy).then_inc(pt_a, 1)
                if it < len(steps):
                    b, j, u, tiles = steps[it]
                    x = smx[:, it % 2, :]
                    act.wait_ge(s_max, it + 1)
                    nc.scalar.activation(prob[it % 2][:, 0:len(tiles) * P], s_bank(it)[:, 0:len(tiles) * P], ACT.Exp,
                                         bias=x[:, 1:2], accum_out=x[:, 2:3])
                    head = j + 4 * u
                    nc.scalar.activation(x[:, 3:4], sink[:, head:head + 1], ACT.Exp, bias=x[:, 1:2]).then_inc(s_exp, 1)
                if it >= 3 and steps[it - 3][2] == 1:
                    b, j, u, tiles = steps[it - 3]
                    act.wait_ge(pv_ready, it - 2)
                    nc.scalar.activation(at_hi[:, b, j, :], ps[:, o_bank(it - 3), 0:P], ACT.Copy).then_inc(ao_hi, 1)

            def out_takes(t):
                per = [(unit_ready[b], 4) for b in range(3)] + [(unit_free[b], 4) for b in range(3)]
                with T.loop(act, 2, per) as i:
                    for s in range(4):
                        for n in range(GROUPS):
                            act.wait_ge(unit_ready[n], T.next(unit_ready[n]))
                            act.sem_inc(act_gate, 1)
                            nc.scalar.activation(t[:, 3 * n:3 * n + 3, bass.ds(i * 4 + s, 1), :],
                                                 ps[:, n, 0:GN].rearrange("p (t o n) -> p t o n", t=GT, o=1),
                                                 ACT.Copy).then_inc(unit_free[n], 1)
                            T.add(unit_free[n])
                for b in range(3):
                    act.wait_ge(unit_free[b], T.last(unit_free[b]))

            def mlp_hidden(p):
                for f in range(2):
                    for n in range(GROUPS):
                        x = relu[(f * 3 + n) % 2]
                        act.wait_ge(sq_done, T.next(sq_done))
                        take(x[:], n, ACT.Relu)
                        act.wait_ge(unit_free[n], T.last(unit_free[n]))
                        nc.scalar.activation(hidden[p][0][:, f, GN * n:GN * (n + 1)], x[:], ACT.Square).then_inc(hid_hi, 1)
                        T.add(hid_hi)

            def mlp():
                act.wait_ge(n_lo, T.last(n_lo))
                act.wait_ge(x_stored, T.last(x_stored))
                mlp_hidden(0)
                per = [(unit_ready[b], 4) for b in range(3)] + [(unit_free[b], 4) for b in range(3)]
                with T.loop(act, (PAIRS - 2) // 2, per + [(sq_done, 12), (hid_hi, 12)]):
                    for p in (1, 0):
                        mlp_hidden(p)
                mlp_hidden(1)
                for b in range(4):
                    acc[b] += PAIRS * 2 * GROUPS
                    act.wait_ge(acc_free[b], acc[b])

            acc = [9, 9, 1, 1]
            for b, n in enumerate((3, 3, 2, 2)):
                acc[b] += n
            out_takes(t_b)
            both_norms(t_b, h_ac[0], 0, 3)
            mlp()
            if STAGE < 2:
                both_norms(t_b, None, 0, 0, final=True)
                act.wait_ge(y_out, 64)
                act.wait_ge(cache_out, 32)
                return
            both_norms(t_b, h_ac[0], 1, 0)

            for n in range(GROUPS):
                act.wait_ge(unit_ready[n], T.next(unit_ready[n]))
                nc.scalar.activation(r_t[:, GN * n:GN * (n + 1)], ps[0:2 * RANK, n, 0:GN], ACT.Copy).then_inc(unit_free[n], 1)
                T.add(unit_free[n])
            act.wait_ge(n_lo, T.last(n_lo))
            act.wait_ge(x_stored, T.last(x_stored))
            for dst, scale in ((gq, P ** -0.5), (gk, 1.0)):
                for h in range(GH):
                    for n in range(GROUPS):
                        take(dst[:, 3 * n:3 * n + 3, h, :], n, scale=scale)
            per = [(unit_ready[b], 4) for b in range(3)] + [(unit_free[b], 4) for b in range(3)]
            for b in range(4):
                T.n[acc_free[b].name] = acc[b]
            with T.loop(act, 2, per + [(acc_free[b], 3) for b in range(4)]):
                for u in range(12):
                    if u < 2:
                        act.wait_ge(acc_free[u + 2], T.last(acc_free[u + 2]))
                    else:
                        act.wait_ge(acc_free[(u - 2) % 4], T.next(acc_free[(u - 2) % 4]))
                    take(v_tmp[u % 2][:], u % 3)
                for b in (2, 3):
                    T.add(acc_free[b])
            act.wait_ge(acc_free[2], T.last(acc_free[2]))
            act.wait_ge(acc_free[3], T.last(acc_free[3]))
            for n in range(3):
                act.sem_inc(og_out[n], 16)
            og_rows = og_d.rearrange("t p (c n) -> c p t n", c=DC)
            with T.loop(act, 2, per + [(og_out[n], 64) for n in range(3)] + [(act_own, 12)]) as i:
                for s in range(4):
                    for n in range(GROUPS):
                        act.wait_ge(og_out[n], T.next(og_out[n], 16))
                        take(og_s[n][:], n, ACT.Silu)
                        act.wait_ge(unit_free[n], T.last(unit_free[n]))
                        own(nc.scalar.activation(og_s[n][:], og_s[n][:], ACT.Copy, scale=vec2[:, 72 + s % 2:73 + s % 2]))
                        act.dma_start(og_rows[i * 4 + s][:, 3 * n:3 * n + 3, :],
                                      og_s[n][:].rearrange("p (t n) -> p t n", t=GT)).then_inc(og_out[n], 16)

            for b in range(3):
                act.wait_ge(unit_free[b], T.last(unit_free[b]))
            act.wait_ge(dve_set, 4)
            for d in range(2):
                act.dma_start(gw[RANK * d:RANK * (d + 1), d, :], io["gla_gate_w"][0, d]).then_inc(gla_in, 16)
            n_g = 0
            for d in range(2):
                for h in range(GH):
                    for n in range(GROUPS):
                        x, l = g_x[n_g % 2], g_l[n_g % 2]
                        if n_g >= 2:
                            act.wait_ge(g_sum, n_g - 1)
                        take(x[:], n, ACT.Identity, bias=vec2[:, 64 + 4 * d + h:65 + 4 * d + h])
                        act.wait_ge(unit_free[n], T.last(unit_free[n]))
                        own(nc.scalar.activation(l[:], x[:], ACT.Abs))
                        own(nc.scalar.activation(l[:], l[:], ACT.Exp, scale=-1.0))
                        nc.scalar.activation(l[:], l[:], ACT.Ln, bias=1.0).then_inc(g_ln, 1)
                        n_g += 1
            act.wait_ge(g_sum, n_g)
            act.dma_start(masks[:], io["c_masks"]).then_inc(mask_in, 16)
            nc.scalar.activation(dec[:, 0:TILES, :], bc_f[:, :, :, P - 1], ACT.Exp, scale=1 / GATE_NORM)
            nc.scalar.activation(dec[:, TILES:2 * TILES, :], tot_b[:], ACT.Exp, scale=1 / GATE_NORM).then_inc(dec_ready, 1)

            order = terms()
            state = {"rel": 0, "upd": 0, "ob": 0}

            def exp_term(i):
                kind, d, tile, level = order[i]
                e = ee[i % 2]
                if i >= 2:
                    act.wait_ge(xt_ready, i - 1)
                if relative(kind, d):
                    state["rel"] += 1
                    act.wait_ge(d_ready, state["rel"])
                    x = dd[(state["rel"] - 1) % 2]
                if kind == "pair":
                    a, b = halves(x[:], level), halves(e[:], level)
                    nc.scalar.activation(b[:, :, 0, :], a[:, :, 0, :], ACT.Exp, scale=-1 / GATE_NORM)
                    nc.scalar.activation(b[:, :, 1, :], a[:, :, 1, :], ACT.Exp, scale=1 / GATE_NORM).then_inc(e_ready, 1)
                elif relative(kind, d):
                    nc.scalar.activation(e[:], x[:], ACT.Exp, scale=-1 / GATE_NORM).then_inc(e_ready, 1)
                else:
                    nc.scalar.activation(e[:], (bc_b if d else bc_f)[:, tile], ACT.Exp, scale=1 / GATE_NORM).then_inc(e_ready, 1)

            def turn_k():
                state["upd"] += 1
                act.wait_ge(khn_t, state["upd"])
                if state["upd"] > 1:
                    act.wait_ge(upd_ready, state["upd"] - 1)
                nc.scalar.activation(khn[:].rearrange("p h n -> p (h n)"), ps[:, 2, :], ACT.Copy).then_inc(khn_ready, 1)

            def swap_state(count, dst, src):
                act.wait_ge(st_ready, count)
                act.dma_start(dst[0, 0].rearrange("h k v -> k h v"), st[:]).then_inc(st_out, 16)
                act.wait_ge(st_out, 16 if dst is io["new_state_bwd"] else 32)
                act.dma_start(st[:], src[0, 0].rearrange("h k v -> k h v")).then_inc(st_in, 16)

            i = 0
            exp_term(0)
            i = 1
            turn_k()
            swap_state(1, io["new_state_bwd"], io["state_bwd"])
            for tile in range(TILES - 1, 0, -1):
                if tile != 1:
                    exp_term(i)
                    i += 1
                exp_term(i)
                i += 1
                if tile != 1:
                    turn_k()
                state["ob"] += 1
                act.wait_ge(ob_ready, state["ob"])
                nc.scalar.activation(o_b[:, tile, :], psf[:, 3 * 512:5 * 512], ACT.Copy).then_inc(ob_taken, 1)

            def load_og(tile):
                if tile >= 2:
                    act.wait_ge(ot_taken, 2 * (tile - 1))
                act.dma_start(og[tile % 2][:].rearrange("p c n -> p (c n)"), og_d[tile]).then_inc(og_in[tile % 2], 16)

            def head_norm(tile):
                act.wait_ge(o_sum, tile + 1)
                for h in range(GH):
                    own(nc.scalar.activation(junk[:], oo[:, h * DV:(h + 1) * DV], ACT.Square, accum_out=rs4[:, 0, h:h + 1]))
                nc.scalar.activation(rs4[:, 1, :], rs4[:, 0, :], ACT.Sqrt, bias=eps[:, 0:1], scale=1.0 / DV).then_inc(o_sq, 1)

            def gated_hi(tile):
                act.wait_ge(ot_taken, 2 * (tile + 1))
                nc.scalar.activation(m_hi[:, tile], mm_[:], ACT.Copy).then_inc(gm_hi, 1)

            for n in range(3):
                act.wait_ge(og_out[n], T.next(og_out[n], 16))
            for tile in range(TILES):
                if tile < 2:
                    load_og(tile)
                if tile >= 2:
                    act.wait_ge(o_ready, tile - 1)
                act.wait_ge(gram_ready, 15 * tile + 1)
                nc.scalar.activation(att[tile % 2][:].rearrange("p h n -> p (h n)"), ps[:, (15 * tile) % 2, :], ACT.Copy,
                                     scale=2.0).then_inc(diag_ready, 1)
                for j in range(14):
                    exp_term(i)
                    i += 1
                    if tile and j == 1:
                        head_norm(tile - 1)
                    if tile and j == 8:
                        gated_hi(tile - 1)
                        if tile + 1 < TILES:
                            load_og(tile + 1) if tile + 1 >= 2 else None
                if tile:
                    exp_term(i)
                    i += 1
                if tile < TILES - 1:
                    exp_term(i)
                    i += 1
                    turn_k()
                if tile == 0:
                    swap_state(9, io["new_state_fwd"], io["state_fwd"])
            head_norm(TILES - 1)
            gated_hi(TILES - 1)
            act.wait_ge(gm_lo, TILES)
            act.sem_inc(gla_free, 1)

            out_takes(t_a)
            both_norms(t_a, h_bc[0], 1, 3)
            for b in range(4):
                acc[b] = T.last(acc_free[b])
            mlp()
            both_norms(t_a, None, 1, 0, final=True)
            act.wait_ge(y_out, 64)
            act.wait_ge(cache_out, 32)
            act.wait_ge(st_out, 32)

        @block.vector
        def _(dve):
            T = Tally()
            V = nc.vector

            def own(ins):
                ins.then_inc(dve_own, 1)
                dve.wait_ge(dve_own, T.next(dve_own))

            V.memset(ones[:], 1.0).then_inc(dve_set, 1)
            V.memset(eps[:], EPS).then_inc(dve_set, 1)
            dve.wait_ge(hi_split, 1)
            for b in range(4):
                dve.sem_inc(acc_free[b], 1)
                T.add(acc_free[b])
            dve.sem_inc(sq_done, 2)
            T.add(sq_done, 2)
            dve.sem_inc(conv_m, 3)
            dve.sem_inc(conv_y, 1)
            T.add(conv_m, 3)
            T.add(conv_y, 1)

            def full(t, n):
                return t[:, 3 * n:3 * n + 3]

            dve.wait_ge(vec_turned, 1)
            V.tensor_copy(vec1[:, 0:124], ps[:, 7, 0:124]).then_inc(vec_copied, 1)
            V.tensor_copy(vec2[:, 0:74], ps[:, 7, P:P + 74]).then_inc(vec_copied, 1)
            dve.wait_ge(vec_copied, 2)
            for layer in range(2):
                bias = vec1[:, 48 * layer:48 * (layer + 1)].rearrange("p (a c) -> p a c", c=DC).unsqueeze(3)
                last = V.tensor_copy(mods[:, layer], bias.broadcast_to([P, KINDS, DC, 2]))
            own(last)
            for layer in range(2):
                with T.loop(dve, DC // 2, [(acc_ready[b], 1) for b in range(2)] + [(acc_free[b], 1) for b in range(2)]):
                    for b in range(2):
                        dve.wait_ge(acc_ready[b], T.next(acc_ready[b]))
                        dve.wait_ge(acc_free[1 - b], T.last(acc_free[1 - b]))
                        m = mods[:, layer].rearrange("p a c k -> p (a c k)")
                        V.tensor_tensor(m, ps[:, 3 + b, 0:96], m, ALU.add).then_inc(acc_free[b], 1)
                        T.add(acc_free[b])
            dve.wait_ge(acc_free[1], T.last(acc_free[1]))
            for layer in range(2):
                for kind, norm, plus in ((1, 0, 1.0), (2, 1, 0.0), (4, 2, 1.0), (5, 3, 0.0)):
                    g = vec2[:, 32 * layer + 8 * norm:32 * layer + 8 * (norm + 1)].unsqueeze(2).broadcast_to([P, DC, 2])
                    last = V.scalar_tensor_tensor(out=mods[:, layer, kind], in0=mods[:, layer, kind], scalar=plus, in1=g,
                                                  op0=ALU.add, op1=ALU.mult)
            last.then_inc(mods_ready, 1)
            dve.wait_ge(mods_ready, 1)

            def spread(n_tiles=GT):
                return rt[:].rearrange("p (t n) -> p t n", t=GT).unsqueeze(2).broadcast_to([P, GT, DC, P])

            def root_mean():
                dve.wait_ge(n_sq, T.next(n_sq))
                V.tensor_reduce(ss[:].rearrange("p (t n) -> p t n", t=GT), sq[:].rearrange("p t c n -> p t n c"),
                                AX_X, ALU.add).then_inc(n_ss, 1)
                dve.wait_ge(n_rt, T.next(n_rt))
                own(V.reciprocal(rt[:], rt[:]))

            def normed(n, t, src, lo, hi):
                root_mean()
                V.tensor_tensor(full(t, n), src[:], spread(), ALU.mult).then_inc(n_xn, 1)
                dve.wait_ge(n_hi, T.next(n_hi))
                V.tensor_tensor(full(lo, n), sq[:], full(hi, n).bitcast(F32), ALU.subtract).then_inc(n_lo, 1)
                T.add(n_lo)

            for n in range(GROUPS):
                normed(n, t_b, xb[n % 2], h_ac[1], h_ac[0])

            def both_norms(t, h, layer, gate, clear=False, final=False):
                for n in range(GROUPS):
                    root_mean()
                    own(V.tensor_tensor(full(t, n), full(t, n), spread(), ALU.mult))
                    dve.wait_ge(x_loaded[n % 2], T.next(x_loaded[n % 2], 16))
                    for c in range(DC):
                        for lo, up, cond in ([(0, 1, 0), (1, 3, 1)] if n == 0 else [(0, 3, 1)]):
                            last = V.scalar_tensor_tensor(out=xb[n % 2][:, lo:up, c, :], in0=t[:, 3 * n + lo:3 * n + up, c, :],
                                                          scalar=mods[:, layer, gate, c, cond:cond + 1],
                                                          in1=xb[n % 2][:, lo:up, c, :], op0=ALU.mult, op1=ALU.add)
                    last.then_inc(n_x, 1)
                    dve.wait_ge(n_x, T.next(n_x))
                    if not final:
                        normed(n, t, xb[n % 2], h[1], h[0])
                        if clear:
                            own(V.memset(full(t, n), 0.0))

            dve.wait_ge(x_stored, 16 * GROUPS)
            V.memset(u_cv[:], 0.0).then_inc(u_clear, 1)
            dve.wait_ge(u_clear, 1)
            for b in range(3):
                T.add(unit_free[b], 1 + 8)
            per = [(unit_free[b], 3) for b in range(3)] + [(conv_u, 3), (conv_y, 1), (conv_m, 3), (dve_own, 9)]
            with T.loop(dve, CC, per) as i:
                dve.wait_ge(conv_y, T.last(conv_y))
                own(V.tensor_tensor(cw[:].unsqueeze(2), vec1[:, 112:124].rearrange("p (w c) -> p w c", w=3)[:, :, bass.ds(i, 1)],
                                    one1[:].unsqueeze(1).broadcast_to([P, 3, 1]), ALU.mult))
                for n in range(GROUPS):
                    dve.wait_ge(unit_free[n], T.next(unit_free[n], 2))
                    for d0, s0, m in ([(1, 0, P), (P + 3, P, GN - P)] if n == 0 else [(GN * n + 3, GN * n, GN)]):
                        last = V.tensor_tensor(u_cv[:, d0:d0 + m], u_cv[:, d0:d0 + m], c_cv[:, s0:s0 + m], ALU.mult)
                    last.then_inc(conv_u, 1)
                    T.add(conv_u)
                dve.wait_ge(conv_u, T.last(conv_u))
                own(V.tensor_scalar(y_cv[:], u_cv[:, 0:1154], cw[:, 0:1], None, ALU.mult))
                own(V.scalar_tensor_tensor(out=y_cv[:], in0=u_cv[:, 1:1155], scalar=cw[:, 1:2], in1=y_cv[:],
                                           op0=ALU.mult, op1=ALU.add))
                V.scalar_tensor_tensor(out=y_cv[:], in0=u_cv[:, 2:1156], scalar=cw[:, 2:3], in1=y_cv[:],
                                       op0=ALU.mult, op1=ALU.add).then_inc(conv_y, 1)
                dve.wait_ge(conv_y, T.next(conv_y))
                for n in range(GROUPS):
                    dve.wait_ge(unit_free[n], T.next(unit_free[n]))
                    m = m_f[n % 2]
                    dve.wait_ge(conv_m, T.last(conv_m))
                    if n == 0:
                        V.tensor_tensor(m[:, 0:P], y_cv[:, 0:P], c_cv[:, 0:P], ALU.mult)
                        own(V.tensor_tensor(m[:, P:GN], y_cv[:, P + 2:GN + 2], c_cv[:, P:GN], ALU.mult))
                    else:
                        own(V.tensor_tensor(m[:], y_cv[:, GN * n + 2:GN * (n + 1) + 2], c_cv[:, GN * n:GN * (n + 1)], ALU.mult))
                    v = m[:].rearrange("p (t o n) -> p t o n", t=GT, o=1)
                    hi = conv_hi[:, 3 * n:3 * n + 3, bass.ds(i, 1), :]
                    own(V.tensor_tensor(hi, v, one1[:].unsqueeze(2).unsqueeze(3).broadcast_to([P, GT, 1, P]), ALU.mult))
                    V.tensor_tensor(conv_lo[:, 3 * n:3 * n + 3, bass.ds(i, 1), :], v, hi.bitcast(F32),
                                    ALU.subtract).then_inc(conv_m, 1)
                    T.add(conv_m)
            dve.wait_ge(conv_m, T.last(conv_m))

            dve.wait_ge(att_in, 96)
            r = 0
            for t in [k_t[:]] + [q_t[:, j, :] for j in range(4)]:
                for half in range(2):
                    b = r % 4
                    dve.wait_ge(acc_ready[b], T.next(acc_ready[b]))
                    x = t[:, P + 512 * half:P + 512 * (half + 1)]
                    a = slice(512 * half, 512 * (half + 1))
                    V.tensor_tensor(rt2[:], ps[:, 3 + b, :], sinT[:, a], ALU.mult).then_inc(acc_free[b], 1)
                    own(V.tensor_tensor(rt1[:], x, cosT[:, a], ALU.mult))
                    dve.wait_ge(acc_free[b], T.next(acc_free[b]))
                    V.tensor_tensor(x, rt1[:], rt2[:], ALU.add).then_inc(rope_done, 1)
                    r += 1
                    dve.wait_ge(rope_done, r)

            steps = attention_steps()
            for it in range(len(steps) + 3):
                if 2 <= it < len(steps) + 2:
                    b, j, u, tiles = steps[it - 2]
                    if len(tiles) > 3:
                        dve.wait_ge(pt_ready, it - 1)
                        if it >= 4:
                            dve.wait_ge(pv_ready, it - 3)
                        m = len(tiles) - 3
                        V.tensor_copy(prT[it % 2][:, 3:3 + m, :],
                                      ps[:, 1, 0:m * P].rearrange("p (t n) -> p t n", t=m)).then_inc(pt_v, 1)
                if it < len(steps):
                    b, j, u, tiles = steps[it]
                    x = smx[:, it % 2, :]
                    s = s_bank(it)
                    dve.wait_ge(s_ready, it + 1)
                    last = None
                    for pos, (what, tile) in enumerate(tiles):
                        if what == "own" and b and tile != b:
                            cols = s[:, pos * P:(pos + 1) * P]
                            last = V.tensor_tensor(cols, cols, band[:, 0 if tile < b else 1, :], ALU.add)
                    if last is not None:
                        own(last)
                    own(V.tensor_reduce(x[:, 0:1], s[:, 0:len(tiles) * P], AX_X, ALU.max))
                    head = j + 4 * u
                    V.tensor_scalar(x[:, 1:2], x[:, 0:1], sink[:, head:head + 1], -1.0, ALU.max, ALU.mult).then_inc(s_max, 1)
                if 1 <= it <= len(steps):
                    b, j, u, tiles = steps[it - 1]
                    x = smx[:, (it - 1) % 2, :]
                    dve.wait_ge(s_exp, it)
                    own(V.tensor_tensor(x[:, 4:5], x[:, 2:3], x[:, 3:4], ALU.add))
                    own(V.reciprocal(x[:, 5:6], x[:, 4:5]))
                    pr = prob[(it - 1) % 2][:, 0:len(tiles) * P]
                    V.tensor_scalar(pr, pr, x[:, 5:6], None, ALU.mult).then_inc(s_norm, 1)
                    dve.wait_ge(s_norm, it)
                if it >= 3 and steps[it - 3][2] == 1:
                    b, j, u, tiles = steps[it - 3]
                    n_pair = (it - 3) // 2 + 1
                    dve.wait_ge(ao_hi, n_pair)
                    V.tensor_tensor(at_lo[:, b, j, :], ps[:, o_bank(it - 3), 0:P], at_hi[:, b, j, :].bitcast(F32),
                                    ALU.subtract).then_inc(ao_lo, 1)

            both_norms(t_b, h_ac, 0, 2, clear=True)

            def mlp_hidden(p):
                for f in range(2):
                    for n in range(GROUPS):
                        u = (f * 3 + n) % 2
                        dve.wait_ge(unit_free[n], T.next(unit_free[n]))
                        if T.n.get(hid_lo.name):
                            dve.wait_ge(hid_lo, T.last(hid_lo))
                        V.tensor_tensor(sqr[u][:], relu[u][:], relu[u][:], ALU.mult).then_inc(sq_done, 1)
                        dve.wait_ge(sq_done, T.next(sq_done))
                        dve.wait_ge(hid_hi, T.next(hid_hi))
                        V.tensor_tensor(hidden[p][1][:, f, GN * n:GN * (n + 1)], sqr[u][:],
                                        hidden[p][0][:, f, GN * n:GN * (n + 1)].bitcast(F32),
                                        ALU.subtract).then_inc(hid_lo, 1)
                        T.add(hid_lo)

            def mlp_sum(t):
                for n in range(GROUPS):
                    for c in range(DC):
                        b = c % 4
                        dve.wait_ge(acc_ready[b], T.next(acc_ready[b]))
                        x = t[:, 3 * n:3 * n + 3, c, :]
                        V.tensor_tensor(x, ps[:, 3 + b, 0:GN].rearrange("p (t n) -> p t n", t=GT), x,
                                        ALU.add).then_inc(acc_free[b], 1)
                        T.add(acc_free[b])

            def mlp(t):
                dve.wait_ge(n_lo, T.last(n_lo))
                mlp_hidden(0)
                per = [(unit_free[b], 4) for b in range(3)] + [(sq_done, 12), (hid_hi, 12), (hid_lo, 12)]
                per += [(acc_ready[b], 12) for b in range(4)] + [(acc_free[b], 12) for b in range(4)]
                with T.loop(dve, (PAIRS - 2) // 2, per):
                    for p in (1, 0):
                        mlp_hidden(p)
                        mlp_sum(t)
                mlp_hidden(1)
                mlp_sum(t)
                mlp_sum(t)
                for b in range(4):
                    dve.wait_ge(acc_free[b], T.last(acc_free[b]))

            for b, turned in enumerate((2, 1, 1)):
                T.add(unit_free[b], 6 + turned + 8)
            mlp(t_b)
            if STAGE < 2:
                both_norms(t_b, None, 0, 5, final=True)
                return
            both_norms(t_b, h_ac, 0, 5)

            with T.loop(dve, 2, [(acc_ready[b], 3) for b in range(4)] + [(acc_free[b], 3) for b in range(4)]) as i:
                for u in range(12):
                    b, n = u % 4, u % 3
                    dve.wait_ge(acc_ready[b], T.next(acc_ready[b]))
                    V.tensor_scalar(gv[:, 3 * n:3 * n + 3, bass.ds(i * 512 + (u // 3) * P, P)],
                                    ps[:, 3 + b, 0:GN].rearrange("p (t n) -> p t n", t=GT), 1.0, None,
                                    ALU.mult).then_inc(acc_free[b], 1)
                    T.add(acc_free[b])

            for b in range(3):
                dve.wait_ge(unit_free[b], T.next(unit_free[b], 1 + 8 + 8 + 8))
            V.memset(gw[:], 0.0).then_inc(dve_set, 1)
            V.memset(bc_b[:, :, :, 0:1], 0.0).then_inc(dve_set, 1)
            dve.wait_ge(dve_set, 4)
            n_g = 0
            for d in range(2):
                for h in range(GH):
                    for n in range(GROUPS):
                        g = g_g[n_g % 2]
                        dve.wait_ge(g_ln, n_g + 1)
                        own(V.scalar_tensor_tensor(out=g[:], in0=g_x[n_g % 2][:], scalar=0.0, in1=g_l[n_g % 2][:],
                                                   op0=ALU.min, op1=ALU.subtract))
                        for t in range(GT):
                            tile = 3 * n + t
                            if d == 0:
                                last = V.tensor_tensor_scan(bc_f[:, tile, h, :], ones[:], g[:, t * P:(t + 1) * P], 0.0,
                                                            ALU.mult, ALU.add)
                            else:
                                last = V.tensor_tensor_scan(bc_b[:, tile, h, 1:P], ones[:, 0:P - 1],
                                                            g[:, t * P:(t + 1) * P - 1], 0.0, ALU.mult, ALU.add)
                        if d:
                            own(last)
                            last = V.tensor_tensor(tot_b[:, 3 * n:3 * n + 3, h:h + 1], bc_b[:, 3 * n:3 * n + 3, h, P - 1:P],
                                                   g[:].rearrange("p (t n) -> p t n", t=GT)[:, :, P - 1:P], ALU.add)
                        last.then_inc(g_sum, 1)
                        n_g += 1
                        dve.wait_ge(g_sum, n_g)
            for b in range(3):
                T.add(unit_free[b], 8)

            order = terms()
            count = {"pair": 0, "st": 0, "upd": 0}

            def term(i):
                kind, d, tile, level = order[i]
                e = ee[i % 2]
                dve.wait_ge(e_ready, i + 1)
                if kind == "pair":
                    j = count["pair"]
                    count["pair"] += 1
                    if j >= 2:
                        k = j - 2
                        dve.wait_ge(gram_ready, 15 * (k // 14) + 2 + k % 14)
                    x = halves(xx[j % 2][:], level)
                    a, b = (gq, gk) if d else (gk, gq)
                    V.tensor_tensor(x[:, :, 0, :], halves(a[:, tile], level)[:, :, 0, :], halves(e[:], level)[:, :, 0, :], ALU.mult)
                    V.tensor_tensor(x[:, :, 1, :], halves(b[:, tile], level)[:, :, 1, :], halves(e[:], level)[:, :, 1, :],
                                    ALU.mult).then_inc(xt_ready, 1)
                else:
                    if kind == "k" and count["upd"]:
                        dve.wait_ge(khn_t, count["upd"])
                    if kind == "k":
                        count["upd"] += 1
                    if kind == "q":
                        if d and tile < TILES - 1:
                            dve.wait_ge(ob_ready, TILES - 1 - tile)
                        elif not d and tile > 1:
                            dve.wait_ge(o_ready, tile)
                        elif not d:
                            dve.wait_ge(ob_ready, TILES - 1)
                    V.tensor_tensor((kh if kind == "k" else qh)[:], (gk if kind == "k" else gq)[:, tile], e[:],
                                    ALU.mult).then_inc(xt_ready, 1)

            def update(d, tile):
                count["st"] += 1
                dve.wait_ge(upd_ready, count["st"])
                if tile == 0:
                    V.tensor_copy(st[:].rearrange("p h v -> p (h v)"), psf[:, 5 * 512:7 * 512]).then_inc(st_ready, 1)
                else:
                    for h in range(GH):
                        last = V.scalar_tensor_tensor(out=st[:, h, :], in0=st[:, h, :],
                                                      scalar=dec[:, TILES * d + tile, h:h + 1],
                                                      in1=psf[:, 5 * 512 + DV * h:5 * 512 + DV * (h + 1)],
                                                      op0=ALU.mult, op1=ALU.add)
                    last.then_inc(st_ready, 1)
                dve.wait_ge(st_ready, count["st"])

            dve.wait_ge(dec_ready, 1)
            i = 0
            for tile in [0] + list(range(TILES - 1, 0, -1)):
                for _ in range((tile != 1) + (tile != 0)):
                    term(i)
                    i += 1
                if tile == TILES - 1:
                    dve.wait_ge(st_in, 16)
                if tile != 1:
                    update(1, tile)

            def head_scale(tile):
                dve.wait_ge(o_sq, tile + 1)
                own(V.reciprocal(rs4[:, 1, :], rs4[:, 1, :]))
                o3 = oo[:].rearrange("p (h v) -> p h v", h=GH)
                V.tensor_tensor(o3, o3, rs4[:, 1, :].unsqueeze(2).broadcast_to([P, GH, DV]), ALU.mult).then_inc(o_nrm, 1)

            def gate_half(tile, half):
                dve.wait_ge(ot_ready, 2 * tile + half + 1)
                if half == 0:
                    dve.wait_ge(og_in[tile % 2], 16 * (tile // 2 + 1))
                    if tile:
                        dve.wait_ge(gm_lo, tile)
                V.tensor_tensor(mm_[:, 4 * half:4 * half + 4, :], ps[:, 7, :].rearrange("p (c n) -> p c n", c=4),
                                og[tile % 2][:, 4 * half:4 * half + 4, :], ALU.mult).then_inc(ot_taken, 1)

            def gated_lo(tile):
                dve.wait_ge(gm_hi, tile + 1)
                V.tensor_tensor(m_lo[:, tile], mm_[:], m_hi[:, tile].bitcast(F32), ALU.subtract).then_inc(gm_lo, 1)

            def place(tile, jj):
                dve.wait_ge(gram_ready, 15 * tile + 2 + jj)
                if jj == 0:
                    dve.wait_ge(diag_ready, tile + 1)
                    dve.wait_ge(mask_in, 16)
                else:
                    dve.wait_ge(gram_taken, 14 * tile + jj)
                level, d = jj // 2, jj % 2
                V.copy_predicated(att[tile % 2][:], masks[:, 2 * level + d, :].bitcast(mybir.dt.int32).unsqueeze(1).broadcast_to([P, GH, P]),
                                  ps[:, (15 * tile + 1 + jj) % 2, :].rearrange("p (h n) -> p h n", h=GH)).then_inc(gram_taken, 1)

            for tile in range(TILES):
                for j in range(14):
                    term(i)
                    i += 1
                    if j:
                        place(tile, j - 1)
                    if tile:
                        if j == 3:
                            head_scale(tile - 1)
                        if j == 5:
                            gate_half(tile - 1, 0)
                        if j == 7:
                            gate_half(tile - 1, 1)
                        if j == 10:
                            gated_lo(tile - 1)
                if tile:
                    term(i)
                    i += 1
                if tile < TILES - 1:
                    term(i)
                    i += 1
                place(tile, 13)
                dve.wait_ge(o_ready, tile + 1)
                if tile:
                    dve.wait_ge(ot_ready, 2 * tile)
                    V.tensor_tensor(oo[:], psf[:, 3 * 512:5 * 512], o_b[:, tile, :], ALU.add).then_inc(o_sum, 1)
                else:
                    V.tensor_copy(oo[:], psf[:, 3 * 512:5 * 512]).then_inc(o_sum, 1)
                if tile == 1:
                    dve.wait_ge(st_in, 32)
                if tile < TILES - 1:
                    update(0, tile)
            head_scale(TILES - 1)
            gate_half(TILES - 1, 0)
            gate_half(TILES - 1, 1)
            gated_lo(TILES - 1)

            both_norms(t_a, h_bc, 1, 2, clear=True)
            for b in range(3):
                T.add(unit_free[b], 8)
            mlp(t_a)
            both_norms(t_a, None, 1, 5, final=True)

        @block.tensor
        def _(pe):
            T = Tally()
            M = nc.tensor
            owed = [1]
            T.add(panel_split, 3)
            pe.sem_inc(panel_used, 2)


            def turn(out, in_):
                n = in_.shape[0]
                return M.transpose(out, in_, ident[0:n, 0:n])

            pe.wait_ge(const_in, 16 * N_CONST)
            turn(ps[:, 7, 0:124], rows1[0:124, :])
            turn(ps[:, 7, P:P + 74], rows2[0:74, :]).then_inc(vec_turned, 1)
            pe.wait_ge(csil_ready, 1)
            for layer in range(2):
                per = [(mod_landed[b], 16) for b in range(2)] + [(acc_free[b], 1) for b in range(2)]
                with T.loop(pe, DC // 2, per) as i:
                    for b in range(2):
                        pe.wait_ge(mod_landed[b], T.next(mod_landed[b], 16))
                        pe.wait_ge(acc_free[b], T.next(acc_free[b]))
                        for f in range(KINDS * DC):
                            last = M.matmul(ps[:, 3 + b, 2 * f:2 * f + 2], mod_w[b][:, f * P:(f + 1) * P],
                                            csil[:, bass.ds(i * 2 + b, 1), :].rearrange("p o k -> p (o k)"),
                                            start=True, stop=True)
                        last.then_inc(acc_ready[b], 1)

            def norm_sum():
                pe.wait_ge(n_ss, T.next(n_ss))
                M.matmul(ps[:, 7, 0:GN], ones[:], ss[:], start=True, stop=True).then_inc(n_sum, 1)

            pe.wait_ge(dve_set, 1)
            for n in range(GROUPS):
                for c in range(DC):
                    bank = (n * DC + c) % 3
                    pe.wait_ge(unit_free[bank], T.next(unit_free[bank]))
                    for t in range(GT):
                        last = turn(ps[:, bank, t * P:(t + 1) * P], x_in[:, 3 * n + t, c * P:(c + 1) * P])
                    last.then_inc(unit_ready[bank], 1)
                if n == 0:
                    pe.wait_ge(vec_copied, 2)
                norm_sum()

            def both_norms(final=False):
                for n in range(GROUPS):
                    norm_sum()
                    if not final:
                        norm_sum()
                        continue
                    pe.wait_ge(n_x, T.next(n_x))
                    for c in range(DC):
                        bank = (n * DC + c) % 3
                        pe.wait_ge(unit_free[bank], T.next(unit_free[bank]))
                        for t in range(GT):
                            last = turn(ps[:, bank, t * P:(t + 1) * P], xb[n % 2][:, t, c, :])
                        last.then_inc(unit_ready[bank], 1)
                if not final:
                    T.add(n_x, 3)

            def project(slot, h, normed=None, hold=False, width=P):
                pe.wait_ge(panel_split, T.next(panel_split))
                for n in range(GROUPS):
                    if normed is not None:
                        pe.wait_ge(n_lo, normed + n + 1)
                    pe.wait_ge(unit_free[n], T.next(unit_free[n]))
                    for c in range(DC):
                        for w, x in ((w_hi, 0), (w_hi, 1), (w_lo, 0)):
                            last = M.matmul(ps[0:width, n, 0:GN], w[:, slot, c, 0:width], h(x, c, n),
                                            start=(c == 0 and x == 0 and w is w_hi), stop=(c == DC - 1 and w is w_lo))
                            if n == 0 and c == 0 and w is w_hi and x == 0 and not hold:
                                last.then_inc(panel_used, owed[0])
                                owed[0] = 0
                    last.then_inc(unit_ready[n], 1)
                owed[0] += 1

            def from_acts(h):
                return lambda x, c, n: h[x][:, 3 * n:3 * n + 3, c, :]

            per3 = [(unit_free[b], 3) for b in range(3)]
            with T.loop(pe, CC, per3 + [(panel_split, 3)]):
                for s in range(3):
                    project(s, from_acts(h_ac), normed=0)
            for s in (0, 1, 2, 0, 1, 2):
                project(s, from_acts(h_ac))
            for n in range(GROUPS):
                pe.wait_ge(unit_free[n], T.next(unit_free[n]))
                for t in range(GT):
                    last = turn(ps[:, n, t * P:(t + 1) * P], v_t[:, (3 * n + t) * P:(3 * n + t + 1) * P])
                last.then_inc(unit_ready[n], 1)
            pe.wait_ge(unit_free[0], T.next(unit_free[0]))
            pe.wait_ge(att_in, 96)
            for t in range(2):
                turn(ps[:, 0, t * P:(t + 1) * P], kc_n[:, t, :])
            turn(ps[:, 0, 2 * P:3 * P], k_t[:, 0:P]).then_inc(unit_ready[0], 1)
            r = 0
            for t in [k_t[:]] + [q_t[:, j, :] for j in range(4)]:
                for half in range(2):
                    b = r % 4
                    pe.wait_ge(acc_free[b], T.next(acc_free[b]))
                    M.matmul(ps[:, 3 + b, :], rot[:], t[:, P + 512 * half:P + 512 * (half + 1)],
                             start=True, stop=True).then_inc(acc_ready[b], 1)
                    r += 1

            for b in range(3):
                pe.wait_ge(unit_free[b], T.last(unit_free[b]) + 1)
            pe.wait_ge(rope_done, 10)
            steps = attention_steps()
            wide = [i for i, st_ in enumerate(steps) if len(st_[3]) > 3]
            for it in range(len(steps) + 2):
                if it < len(steps):
                    b, j, u, tiles = steps[it]
                    if it >= 2:
                        pe.wait_ge(s_exp, it - 1)
                    s = s_bank(it)
                    rows = slice(HD * u, HD * (u + 1))
                    q = q_t[rows, j, b * P:(b + 1) * P]
                    if b == 0:
                        runs = [(0, k_t[rows, 0:P])]
                    else:
                        own_t = [t for what, t in tiles if what == "own"]
                        runs = [(0, kc_t[rows, :]), (2 * P, k_t[rows, own_t[0] * P:(own_t[0] + 2) * P])]
                        if len(own_t) == 3:
                            runs.append((4 * P, k_t[rows, own_t[2] * P:(own_t[2] + 1) * P]))
                    for c0, keys in runs:
                        last = M.matmul(s[:, c0:c0 + keys.shape[1]], q, keys, start=True, stop=True)
                    last.then_inc(s_ready, 1)
                if 1 <= it <= len(steps):
                    b, j, u, tiles = steps[it - 1]
                    pe.wait_ge(s_norm, it)
                    if it >= 2:
                        pe.wait_ge(pt_a, it - 1)
                        n_wide = sum(1 for w in wide if w < it - 1)
                        if n_wide:
                            pe.wait_ge(pt_v, n_wide)
                    for pos in range(len(tiles)):
                        bank, col = (0, pos) if pos < 3 else (1, pos - 3)
                        last = turn(ps[:, bank, col * P:(col + 1) * P], prob[(it - 1) % 2][:, pos * P:(pos + 1) * P])
                    last.then_inc(pt_ready, 1)
                if it >= 2:
                    b, j, u, tiles = steps[it - 2]
                    pe.wait_ge(pt_a, it - 1)
                    n_wide = sum(1 for w in wide if w <= it - 2)
                    if n_wide:
                        pe.wait_ge(pt_v, n_wide)
                    pair = (it - 2) // 2
                    if u == 0 and pair >= 2:
                        pe.wait_ge(ao_lo, pair - 1)
                    cols = slice(HD * u, HD * (u + 1))
                    for pos, (what, tile) in enumerate(tiles):
                        v = v_c[:, tile, cols] if what == "ctx" else v_n[:, tile, cols]
                        last = M.matmul(ps[cols, o_bank(it - 2), 0:P], v, prT[it % 2][:, pos, :],
                                        start=(pos == 0), stop=(pos == len(tiles) - 1))
                    last.then_inc(pv_ready, 1)

            pe.wait_ge(ao_lo, len(steps) // 2)
            pe.wait_ge(conv_m, 3 + 3 * CC)

            def mixed(x, c, n):
                if c < CC:
                    return (conv_hi, conv_lo)[x][:, 3 * n:3 * n + 3, c, :]
                return (at_hi, at_lo)[x][:, 3 * n:3 * n + 3, c - CC, :]

            def out_project(s0, h):
                with T.loop(pe, 2, [(unit_free[b], 4) for b in range(3)] + [(panel_split, 4)]):
                    for s in range(4):
                        project((s0 + s) % SLOTS, h)

            out_project(0, mixed)
            both_norms()

            def down(p, slots):
                pe.wait_ge(panel_split, T.next(panel_split))
                for n in range(GROUPS):
                    pe.wait_ge(hid_lo, T.next(hid_lo, 4 if n == 0 else 1))
                    for c in range(DC):
                        b = c % 4
                        pe.wait_ge(acc_free[b], T.next(acc_free[b]))
                        for f in range(2):
                            if f == 1 and n == 0 and c == 0:
                                pe.wait_ge(panel_split, T.next(panel_split))
                            for w, x in ((w_hi, 0), (w_hi, 1), (w_lo, 0)):
                                first = f == 0 and w is w_hi and x == 0
                                last = M.matmul(ps[:, 3 + b, 0:GN], w[:, slots[f], c, :],
                                                hidden[p][x][:, f, GN * n:GN * (n + 1)],
                                                start=first, stop=(f == 1 and w is w_lo))
                                if first and n == 0 and c == 0:
                                    last.then_inc(panel_used, owed[0])
                                    owed[0] = 0
                        last.then_inc(acc_ready[b], 1)
                owed[0] += 2

            def mlp(h, s0, normed):
                a = [(s0 + s) % SLOTS for s in (0, 1)]
                b = [(s0 + s) % SLOTS for s in (2, 3)]
                project(a[0], from_acts(h), normed=normed)
                project(a[1], from_acts(h), hold=True)
                per = [(unit_free[n], 4) for n in range(3)] + [(acc_free[n], 12) for n in range(4)]
                with T.loop(pe, (PAIRS - 2) // 2, per + [(panel_split, 8), (hid_lo, 12)]):
                    for p in range(2):
                        project(b[0], from_acts(h))
                        project(b[1], from_acts(h))
                        down(p, a)
                project(b[0], from_acts(h))
                project(b[1], from_acts(h))
                down(0, a)
                down(1, b)

            mlp(h_ac, 0, 3)
            if STAGE < 2:
                both_norms(final=True)
                return
            both_norms()
            project(0, from_acts(h_ac), normed=6, width=2 * RANK)
            for part in range(2):
                for s in range(4):
                    project((1 + s) % SLOTS, from_acts(h_ac))
            with T.loop(pe, 2, [(unit_free[b], 4) for b in range(3)] + [(panel_split, 4)] + [(acc_free[b], 3) for b in range(4)]):
                for s in range(4):
                    slot = (1 + s) % SLOTS
                    pe.wait_ge(panel_split, T.next(panel_split))
                    for n in range(GROUPS):
                        pe.wait_ge(unit_free[n], T.next(unit_free[n]))
                        for c in range(DC):
                            for w, x in ((w_hi, 0), (w_hi, 1), (w_lo, 0)):
                                first = c == 0 and w is w_hi and x == 0
                                last = M.matmul(ps[:, n, 0:GN], w[:, slot, c, :], h_ac[x][:, 3 * n:3 * n + 3, c, :],
                                                start=first, stop=(c == DC - 1 and w is w_lo))
                                if first and n == 0:
                                    last.then_inc(panel_used, 1)
                        last.then_inc(unit_ready[n], 1)
                        u = 3 * s + n
                        if u:
                            m = (u - 1) % 3
                            pe.wait_ge(unit_free[m], T.last(unit_free[m]) + 1)
                            b = (u - 1) % 4
                            pe.wait_ge(acc_free[b], T.next(acc_free[b]))
                            for t in range(GT):
                                last = turn(ps[:, 3 + b, t * P:(t + 1) * P], v_tmp[(u - 1) % 2][:, t * P:(t + 1) * P])
                            last.then_inc(acc_ready[b], 1)
                pe.wait_ge(unit_free[2], T.last(unit_free[2]) + 1)
                pe.wait_ge(acc_free[3], T.next(acc_free[3]))
                for t in range(GT):
                    last = turn(ps[:, 6, t * P:(t + 1) * P], v_tmp[1][:, t * P:(t + 1) * P])
                last.then_inc(acc_ready[3], 1)
            out_project(1, from_acts(h_ac))

            pe.wait_ge(gla_in, 32)
            for d in range(2):
                for h in range(GH):
                    for n in range(GROUPS):
                        pe.wait_ge(unit_free[n], T.next(unit_free[n]))
                        M.matmul(ps[:, n, 0:GN], gw[:, d, h * P:(h + 1) * P], r_t[:, GN * n:GN * (n + 1)],
                                 start=True, stop=True).then_inc(unit_ready[n], 1)
            for n in range(3):
                pe.wait_ge(unit_free[n], T.last(unit_free[n]) + 1)
            for b in range(4):
                pe.wait_ge(acc_free[b], T.last(acc_free[b]) + 1)

            order = terms()
            count = {"k": 0, "pair": 0}

            def turn_k(i):
                pe.wait_ge(xt_ready, i + 1)
                count["k"] += 1
                if count["k"] > 1:
                    pe.wait_ge(khn_ready, count["k"] - 1)
                for h in range(GH):
                    last = turn(ps[:, 2, h * P:(h + 1) * P], kh[:, h, :])
                last.then_inc(khn_t, 1)

            def update(tile):
                pe.wait_ge(khn_ready, count["k"])
                if count["k"] > 1:
                    pe.wait_ge(st_ready, count["k"] - 1)
                for h in range(GH):
                    last = M.matmul(psf[:, 5 * 512 + DV * h:5 * 512 + DV * (h + 1)], khn[:, h, :],
                                    gv[:, tile, DV * h:DV * (h + 1)], start=True, stop=True)
                last.then_inc(upd_ready, 1)

            i = 0
            n_ob = 0
            for tile in [0] + list(range(TILES - 1, 0, -1)):
                if tile != 1:
                    turn_k(i)
                    i += 1
                if tile:
                    pe.wait_ge(xt_ready, i + 1)
                    i += 1
                    if n_ob:
                        pe.wait_ge(ob_taken, n_ob)
                        pe.wait_ge(st_ready, 1 + n_ob)
                    else:
                        pe.wait_ge(st_in, 16)
                    for h in range(GH):
                        last = M.matmul(psf[:, 3 * 512 + DV * h:3 * 512 + DV * (h + 1)], qh[:, h, :], st[:, h, :],
                                        start=True, stop=True)
                    last.then_inc(ob_ready, 1)
                    n_ob += 1
                if tile != 1:
                    update(tile)

            def grams(item, stationary, moving):
                if item >= 2:
                    prev = item - 2
                    if prev % 15 == 0:
                        pe.wait_ge(diag_ready, prev // 15 + 1)
                    else:
                        pe.wait_ge(gram_taken, 14 * (prev // 15) + prev % 15)
                for h in range(GH):
                    last = M.matmul(ps[:, item % 2, h * P:(h + 1) * P], stationary[:, h, :], moving[:, h, :],
                                    start=True, stop=True)
                last.then_inc(gram_ready, 1)

            def turn_o(tile, half):
                if half == 0:
                    pe.wait_ge(o_nrm, tile + 1)
                if tile or half:
                    pe.wait_ge(ot_taken, 2 * tile + half)
                for c in range(4):
                    last = turn(ps[:, 7, c * P:(c + 1) * P], oo[:, (4 * half + c) * P:(4 * half + c + 1) * P])
                last.then_inc(ot_ready, 1)

            for tile in range(TILES):
                grams(15 * tile, gk[:, tile], gq[:, tile])
                for jj in range(14):
                    pe.wait_ge(xt_ready, i + 1)
                    i += 1
                    x = xx[jj % 2]
                    grams(15 * tile + 1 + jj, x, x)
                    if tile and jj == 3:
                        turn_o(tile - 1, 0)
                    if tile and jj == 5:
                        turn_o(tile - 1, 1)
                if tile:
                    pe.wait_ge(xt_ready, i + 1)
                    i += 1
                if tile < TILES - 1:
                    turn_k(i)
                    i += 1
                pe.wait_ge(gram_taken, 14 * (tile + 1))
                pe.wait_ge(ob_taken, TILES - 1)
                if tile:
                    pe.wait_ge(o_sum, tile)
                    pe.wait_ge(st_ready, 8 + tile)
                    pe.wait_ge(st_in, 32)
                for h in range(GH):
                    o = psf[:, 3 * 512 + DV * h:3 * 512 + DV * (h + 1)]
                    last = M.matmul(o, att[tile % 2][:, h, :], gv[:, tile, DV * h:DV * (h + 1)], start=True, stop=(tile == 0))
                    if tile:
                        last = M.matmul(o, qh[:, h, :], st[:, h, :], start=False, stop=True)
                last.then_inc(o_ready, 1)
                if tile < TILES - 1:
                    update(tile)
            for half in range(2):
                turn_o(TILES - 1, half)

            pe.wait_ge(gm_lo, TILES)
            out_project(1, lambda x, c, n: (m_hi, m_lo)[x][:, 3 * n:3 * n + 3, c, :])
            both_norms()
            mlp(h_bc, 1, 9)
            both_norms(final=True)


def tables():
    f32 = np.float32
    quarter = HD // 4
    inv = (f32(10000.0) ** (-(np.arange(quarter, dtype=f32) * f32(2.0) / f32(2 * quarter)))).astype(f32)
    pos = np.arange(LAT)
    f = np.arange(P) % HD
    where = np.where((f < HD // 2)[:, None], (pos // 64)[None, :], (pos % 64)[None, :]).astype(f32)
    ang = (where * inv[f % quarter][:, None]).astype(f32)
    rot = np.zeros((P, P), f32)
    for m in range(P):
        if m % (2 * quarter) < quarter:
            rot[m + quarter, m] = -1.0
        else:
            rot[m - quarter, m] = 1.0
    q, key = np.arange(P)[:, None], np.arange(P)[None, :]
    band = np.stack([np.where(key >= q, 0.0, -BAND), np.where(key <= q, 0.0, -BAND)], 1).astype(f32)
    masks = np.zeros((P, 2 * len(LEVELS), P), f32)
    for i, n in enumerate(LEVELS):
        same = (q // (2 * n)) == (key // (2 * n))
        masks[:, 2 * i] = same & (q // n % 2 == 0) & (key // n % 2 == 1)
        masks[:, 2 * i + 1] = same & (q // n % 2 == 1) & (key // n % 2 == 0)
    return {"c_ident": np.eye(P, dtype=f32), "c_cos": np.cos(ang).astype(f32), "c_sin": np.sin(ang).astype(f32),
            "c_rot": rot, "c_band": band, "c_masks": masks}


_INS = ["x_prompt", "x_sample", "cache_k", "cache_v", "state_fwd", "state_bwd", "c", "c_ctx", "mod_w", "mod_b", "norm_g",
        "ab_w_in", "conv_w", "attn_sink", "ab_w_out", "gla_w_in", "gla_gate_w", "gla_gate_b", "gla_norm_g", "gla_w_out",
        "mlp_w1", "mlp_w2"]
_OUTS = [("y_prompt", (1, P, D)), ("y_sample", (1, LAT, D)), ("new_cache_k", (1, 1, P, 2, HD)),
         ("new_cache_v", (1, 1, P, 2, HD)), ("new_state_fwd", (1, 1, GH, P, DV)), ("new_state_bwd", (1, 1, GH, P, DV))]


def kernel(**inputs):
    import concourse.bacc as bacc
    from concourse.bass_utils import run_bass_kernel_spmd

    nc = bacc.Bacc("TRN2", target_bir_lowering=False, num_devices=1)
    arrays = {name: np.ascontiguousarray(inputs[name]) for name in _INS}
    arrays.update(tables())
    io = {name: nc.dram_tensor(name, a.shape, mybir.dt.from_np(a.dtype), kind="ExternalInput").ap()
          for name, a in arrays.items()}
    for name, shape in _OUTS:
        io[name] = nc.dram_tensor(name, shape, F32, kind="ExternalOutput").ap()
    for name in ("x_scratch", "og_scratch"):
        io[name] = nc.dram_tensor(name, (TILES, P, D), F32, kind="Internal").ap()
    build(nc, io)
    got = run_bass_kernel_spmd(nc, [arrays], core_ids=[0]).results[0]
    return tuple(got[name] for name, _ in _OUTS)
```

```python
from contextlib import ExitStack, contextmanager

import numpy as np
import concourse.bass as bass
from concourse import mybir

ALU = mybir.AluOpType
ACT = mybir.ActivationFunctionType
F32 = mybir.dt.float32
F32R = mybir.dt.float32r
U8 = mybir.dt.uint8
AX_X = mybir.AxisListType.X

P = 128
D = 1024
DC = D // P
TILES = 9
TOK = TILES * P
GROUPS = 3
GT = TILES // GROUPS
GN = GT * P
LAT = TOK - P
EPS = 1e-6
KINDS = 6
CONV = D // 2
CC = CONV // P
HD = 64
PAST = 256
FF = 4 * D
PAIRS = FF // P // 2
AB_IN = 2304
GH = 4
DV = 256
RANK = 16
GLA_IN = 3104
GATE_NORM = 16.0
LEVELS = [64, 32, 16, 8, 4, 2, 1]
SLOTS = 4
BAND = 1e30
STAGE = 99


class Tally:

    def __init__(self, start=()):
        self.n = dict(start)
        self.i = None
        self.per = {}

    def last(self, sem, lag=0):
        v = self.n.get(sem.name, 0) - lag
        if self.i is not None and self.per.get(sem.name, 0):
            v = self.i * self.per[sem.name] + v
        return v

    def next(self, sem, n=1):
        self.n[sem.name] = self.n.get(sem.name, 0) + n
        return self.last(sem)

    add = next

    @contextmanager
    def loop(self, eng, times, per):
        per = {s.name: n for s, n in per}
        before = dict(self.n)
        with eng.Fori(0, times) as i:
            self.i, self.per = i, per
            yield i
            self.i, self.per = None, {}
        for name in set(self.n) | set(per):
            grown = self.n.get(name, 0) - before.get(name, 0)
            assert grown == per.get(name, 0), (name, grown, per.get(name, 0))
            self.n[name] = before.get(name, 0) + grown * times


def build(nc, io):
    base = 16512
    Q = TILES * D * 4
    RA, RB, RC, RD = (base + i * Q for i in range(4))
    RW = base + 4 * Q
    PANEL = D * 4
    RS = RW + 3 * SLOTS * PANEL
    RK = RS + 9248

    def at(name, shape, dt, offset):
        return nc.alloc_sbuf_tensor_at(name, shape, dt, offset=offset)

    x_in = at("x_in", [P, TILES, D], F32, RB)
    mod_w = [at(f"mod_w{i}", [P, 2 * D], F32, RA + 8192 * i) for i in range(4)]
    mod_p = [at(f"mod_p{i}", [P, 2, 512], F32, r) for i, r in
             enumerate((RB + 27648, RB + 31744, RW + 2 * PANEL, RW + 3 * PANEL))]
    mod_r = [at(f"mod_r{i}", [4, 512], F32, RS + 2048 * i) for i in range(2)]
    xb = [at(f"xb{n}", [P, GT, DC, P], F32, RD + 12288 * n) for n in range(GROUPS)]

    def acts(name, dt, r, chunks=DC):
        return at(name, [P, TILES, chunks, P], dt, r)

    h_ac = (acts("h_hi_a", F32R, RA), acts("h_lo_c", F32R, RC))
    h_bc = (acts("h_hi_b", F32R, RB), acts("h_lo_c2", F32R, RC))
    sq_a, sq_b, sq_c = (acts(f"sq_{x}", F32, reg) for x, reg in (("a", RA), ("b", RB), ("c", RC)))
    rts = [at(f"rt{i}", [P, GT, P], F32, RS + 1536 * i) for i in range(6)]
    t_b = acts("t_b", F32, RB)
    t_a = acts("t_a", F32, RA)
    hidden = [[at(f"hid{p}{x}", [P, 2, TOK], F32R, RD + 18432 * p + 9216 * x) for x in range(2)] for p in range(2)]
    conv_hi = acts("conv_hi", F32R, RD, CC)
    conv_lo = acts("conv_lo", F32R, RD + Q // 2, CC)
    at_hi = acts("at_hi", F32R, RC, CC)
    at_lo = acts("at_lo", F32R, RC + Q // 2, CC)
    m_hi = acts("m_hi", F32R, RC)
    m_lo = acts("m_lo", F32R, RB)
    q_t = at("q_t", [P, 4, TOK], F32, RB)
    k_t = at("k_t", [P, TOK], F32, RB + 18432)
    v_t = at("v_t", [P, TOK], F32, RB + 23040)
    y_cv = at("y_cv", [P, 1154], F32, RB + 27648)
    m_f = [at(f"m_f{i}", [P, GN], F32, RB + 32288 + 1536 * i) for i in range(2)]
    cw = at("cw", [P, 3], F32, RB + 35392)
    c_cv = at("c_cv", [P, TOK], F32, RS)
    u_cv = at("u_cv", [P, 1156], F32, RS + 4608)
    o = RA
    cosT = at("cosT", [P, LAT], F32, o)
    sinT = at("sinT", [P, LAT], F32, o + 4096)
    v_n = at("v_n", [P, TILES, P], F32, o + 8192)
    kc_n = at("kc_n", [P, 2, P], F32, o + 12800)
    v_c = at("v_c", [P, 2, P], F32, o + 13824)
    kc_t = at("kc_t", [P, 2 * P], F32, o + 14848)
    k_out = at("k_out", [P, P], F32, o + 15872)
    rot = at("rot", [P, P], F32, o + 16384)
    band = at("band", [P, 2, P], F32, o + 16896)
    rt1 = at("rt1", [P, 512], F32, o + 17920)
    rt2 = at("rt2", [P, 512], F32, o + 19968)
    prob = [at(f"prob{i}", [P, 640], F32, o + 22016 + 2560 * i) for i in range(3)]
    prT = [at(f"prT{i}", [P, 5, P], F32, o + 29696 + 2560 * i) for i in range(2)]
    smx = at("smx", [P, 3, 8], F32, o + 34816)
    gq = at("gq", [P, TILES, GH, P], F32, RD)
    gk = at("gk", [P, TILES, GH, P], F32, RD + Q // 2)
    gv = at("gv", [P, TILES, D], F32, RB)
    bc_f = at("bc_f", [P, TILES, GH, P], F32, RA)
    bc_b = at("bc_b", [P, TILES, GH, P], F32, RA + Q // 2)
    o_b = at("o_b", [P, TILES, D], F32, RC)
    v_tmp = [at(f"v_tmp{i}", [P, GN], F32, RS + 1536 * i) for i in range(2)]
    og_s = [at(f"og_s{i}", [P, GN], F32, RS + (0, 1536, 7680)[i]) for i in range(3)]
    r_t = at("r_t", [32, TOK], F32, RS + 3072)
    relu = [at(f"relu{i}", [P, GN], F32, RS + 1536 * i) for i in range(2)]
    sqr = [at(f"sqr{i}", [P, GN], F32, RS + 3072 + 1536 * i) for i in range(2)]
    raw = at("raw", [P, SLOTS, DC, P], F32, RW)
    w_hi = at("w_hi", [P, SLOTS, DC, P], F32R, RW + SLOTS * PANEL)
    w_lo = at("w_lo", [P, SLOTS, DC, P], F32R, RW + 2 * SLOTS * PANEL)
    w = RW
    st = at("st", [P, GH, DV], F32, w)
    dd = [at(f"dd{i}", [P, GH, P], F32, w + 4096 + 2048 * i) for i in range(2)]
    ee = [at(f"ee{i}", [P, GH, P], F32, w + 8192 + 2048 * i) for i in range(2)]
    xx = [at(f"xx{i}", [P, GH, P], F32, w + 12288 + 2048 * i) for i in range(2)]
    qh = at("qh", [P, GH, P], F32, w + 16384)
    kh = at("kh", [P, GH, P], F32, w + 18432)
    khn = at("khn", [P, GH, P], F32, w + 20480)
    att = [at(f"att{i}", [P, GH, P], F32, w + 22528 + 2048 * i) for i in range(2)]
    oo = at("oo", [P, D], F32, w + 26624)
    og = [at(f"og{i}", [P, DC, P], F32, w + 30720 + 4096 * i) for i in range(2)]
    mm_ = at("mm_", [P, DC, P], F32, w + 38912)
    masks = at("masks", [P, 2 * len(LEVELS), P], F32, RS)
    tot_b = at("tot_b", [P, TILES, GH], F32, w + 44800)
    dec = at("dec", [P, 2 * TILES, GH], F32, w + 44960)
    rs4 = at("rs4", [P, 2, GH], F32, w + 45248)
    junk = at("junk", [P, DV], F32, w + 45280)
    gw = at("gw", [32, 2, GH * P], F32, w + 36864)
    g_x = at("g_x", [P, 12, GN], F32, w)
    g_l = at("g_l", [P, 12, GN], F32, w + 18432)
    k = RK
    ident = at("ident", [P, P], F32, k)
    ones = at("ones", [P, P], F32, k + 512)
    vec1 = at("vec1", [P, P], F32, k + 1024)
    vec2 = at("vec2", [P, P], F32, k + 1536)
    mods = at("mods", [P, 2, KINDS, DC, 2], F32, k + 2048)
    csil = at("csil", [P, DC, 2], F32, k + 2816)
    sink = at("sink", [P, 8], F32, k + 2880)
    eps = at("eps", [P, 1], F32, k + 2912)
    one1 = at("one1", [P, 1], F32, k + 2944)
    csr = at("csr", [P, DC, 4], F32R, k + 2976)
    assert k + 3104 <= nc.sbuf_usable_end
    y_sb = at("y_sb", [P, TILES, D], F32, RB)
    rows1 = at("rows1", [P, P], F32, RS)
    rows2 = at("rows2", [P, P], F32, RS + 512)

    x_d = io["x_scratch"]
    og_d = io["og_scratch"]

    with ExitStack() as ctx:
        ps = ctx.enter_context(nc.psum_tensor("ps", [P, 8, 512], F32))
        psf = ps[:, :, :].rearrange("p b n -> p (b n)")

        def sem(name):
            return ctx.enter_context(nc.semaphore(name))

        const_in = sem("const_in")
        xin_in = sem("xin_in")
        mod_landed = [sem(f"mod_landed{i}") for i in range(4)]
        modp_landed = [sem(f"modp_landed{i}") for i in range(4)]
        modp_used = sem("modp_used")
        csr_hi = sem("csr_hi")
        mod_hi = sem("mod_hi")
        mod_lo = sem("mod_lo")
        mod_rows = sem("mod_rows")
        mod_turned = sem("mod_turned")
        mod_added = sem("mod_added")
        raw_landed = [sem(f"raw_landed{i}") for i in range(SLOTS)]
        hi_split = sem("hi_split")
        panel_split = sem("panel_split")
        panel_used = sem("panel_used")
        unit_ready = [sem(f"unit_ready{i}") for i in range(3)]
        unit_free = [sem(f"unit_free{i}") for i in range(3)]
        acc_ready = [sem(f"acc_ready{i}") for i in range(4)]
        acc_free = [sem(f"acc_free{i}") for i in range(4)]
        dve_set = sem("dve_set")
        dve_own = sem("dve_own")
        act_own = sem("act_own")
        vec_turned = sem("vec_turned")
        vec_copied = sem("vec_copied")
        csil_ready = sem("csil_ready")
        mods_ready = sem("mods_ready")
        n_sq = sem("n_sq")
        n_rc = sem("n_rc")
        n_tm = sem("n_tm")
        n_sum = sem("n_sum")
        n_rt = sem("n_rt")
        n_x = sem("n_x")
        n_xn = sem("n_xn")
        n_h = sem("n_h")
        n_hi = sem("n_hi")
        n_lo = sem("n_lo")
        x_stored = sem("x_stored")
        x_loaded = [sem(f"x_loaded{i}") for i in range(GROUPS)]
        t_zero = sem("t_zero")
        sq_done = sem("sq_done")
        hid_hi = sem("hid_hi")
        hid_lo = sem("hid_lo")
        u_clear = sem("u_clear")
        conv_u = sem("conv_u")
        conv_y = sem("conv_y")
        conv_m = sem("conv_m")
        att_in = sem("att_in")
        rope_done = sem("rope_done")
        kv_turned = sem("kv_turned")
        s_ready = sem("s_ready")
        s_max = sem("s_max")
        s_exp = sem("s_exp")
        s_norm = sem("s_norm")
        pt_ready = sem("pt_ready")
        pt_a = sem("pt_a")
        pt_v = sem("pt_v")
        pv_ready = sem("pv_ready")
        ao_hi = sem("ao_hi")
        ao_lo = sem("ao_lo")
        cache_out = sem("cache_out")
        y_out = sem("y_out")
        og_out = [sem(f"og_out{i}") for i in range(3)]
        act_gate = sem("act_gate")
        sp_gate = sem("sp_gate")
        og_in = [sem(f"og_in{i}") for i in range(2)]
        gla_in = sem("gla_in")
        mask_in = sem("mask_in")
        v_tmp_ready = sem("v_tmp_ready")
        g_ln = sem("g_ln")
        g_neg = sem("g_neg")
        g_sum = sem("g_sum")
        d_ready = sem("d_ready")
        e_ready = sem("e_ready")
        xt_ready = sem("xt_ready")
        gram_ready = sem("gram_ready")
        gram_taken = sem("gram_taken")
        diag_ready = sem("diag_ready")
        khn_t = sem("khn_t")
        khn_ready = sem("khn_ready")
        ob_ready = sem("ob_ready")
        ob_taken = sem("ob_taken")
        upd_ready = sem("upd_ready")
        st_ready = sem("st_ready")
        st_in = sem("st_in")
        st_out = sem("st_out")
        o_ready = sem("o_ready")
        o_sum = sem("o_sum")
        o_sq = sem("o_sq")
        o_nrm = sem("o_nrm")
        ot_ready = sem("ot_ready")
        ot_taken = sem("ot_taken")
        gm_hi = sem("gm_hi")
        gm_lo = sem("gm_lo")
        dec_ready = sem("dec_ready")
        gla_free = sem("gla_free")

        block = ctx.enter_context(nc.Block())

        N_CONST = 12
        X_TILES = TILES

        def attention_steps():
            out = []
            for b in range(TILES):
                if b == 0:
                    tiles = [("own", 0)]
                else:
                    tiles = [("ctx", 0), ("ctx", 1)] + [("own", t) for t in (b - 1, b, b + 1) if 1 <= t < TILES]
                out += [(b, j, u, tiles) for j in range(4) for u in range(2)]
            return out

        def s_bank(step):
            return psf[:, (3 + 2 * (step % 2)) * 512:(5 + 2 * (step % 2)) * 512]

        O_BANK, MOD_BANK = 2, 7
        LATE = 2 * KINDS * DC - 2 * DC


        def half_panel(w, k):
            return w[:, 2 + k % 2].rearrange("p c n -> p (c n)").rearrange("p (a n) -> p a n", a=2)

        @block.sync
        def _(sp):
            T = Tally()

            def small(dst, src):
                sp.dma_start(dst, src).then_inc(const_in, 16)

            small(ident[:], io["c_ident"])
            small(rows1[0:96, :], io["mod_b"].rearrange("l (r n) -> (l r) n", n=P))
            small(rows1[96:104, :], io["c_ctx"].rearrange("(r n) -> r n", n=P))
            small(rows1[104:112, :], io["c"].rearrange("b (r n) -> (b r) n", n=P))
            small(rows1[112:124, :], io["conv_w"].rearrange("a w (r n) -> (a w r) n", n=P))
            small(rows2[0:64, :], io["norm_g"].rearrange("l i (r n) -> (l i r) n", n=P))
            small(rows2[64:72, :], io["gla_gate_b"].rearrange("a d (r n) -> (a d r) n", n=P))
            small(rows2[72:74, :], io["gla_norm_g"].rearrange("a (r n) -> (a r) n", n=P))
            small(sink[:], io["attn_sink"].partition_broadcast(P).rearrange("p a h -> p (a h)"))
            small(x_in[:, 0, :], io["x_prompt"][0])
            small(x_in[:, 1:5, :], io["x_sample"][0, 0:512].rearrange("(t p) d -> p t d", p=P))
            small(x_in[:, 5:9, :], io["x_sample"][0, 512:1024].rearrange("(t p) d -> p t d", p=P))

            rows = io["mod_w"][0][:, 0:2 * D].rearrange("(i b p) n -> i b p n", b=4, p=P)
            with T.loop(sp, 2, [(acc_free[b], 1) for b in range(4)]) as i:
                for b in range(4):
                    sp.wait_ge(acc_free[b], T.next(acc_free[b]))
                    sp.sem_inc(sp_gate, 1)
                    sp.dma_start(mod_w[b][:], rows[i, b]).then_inc(mod_landed[b], 16)

            def panel(slot, pieces):
                sp.wait_ge(panel_split, T.next(panel_split))
                sp.sem_inc(sp_gate, 1)
                for dst, src in pieces:
                    sp.dma_start(dst, src).then_inc(raw_landed[slot], 16)

            def columns(w, f):
                return w.rearrange("(k p) (f n) -> f p k n", p=P, n=P)[f]

            w_in = io["ab_w_in"][0]
            with T.loop(sp, CC, [(panel_split, 3)]) as i:
                for s, part in enumerate((1, 2, 0)):
                    src = w_in[:, part * CONV:(part + 1) * CONV]
                    panel(s, [(raw[:, s], columns(src, i))])
            kv = w_in[:, 4 * CONV:4 * CONV + 2 * P]
            for s in range(2):
                panel(s, [(raw[:, s], columns(kv, s))])
            qw = w_in[:, 3 * CONV:4 * CONV].rearrange("(k p) (u j n) -> u j p k n", p=P, u=2, n=HD)
            for j in range(4):
                s = (2 + j) % 3
                panel(s, [(raw[:, s, :, 0:HD], qw[0, j]), (raw[:, s, :, HD:P], qw[1, j])])

            def out_panel(slot, f):
                w_out = io["ab_w_out"][0]
                cols = w_out[0:CONV, :].rearrange("(k p) (f n) -> f p k n", p=P, n=P)
                lo = w_out[CONV:CONV + 4 * HD, :].rearrange("(j p) (f n) -> f p j n", p=HD, n=P)
                hi = w_out[CONV + 4 * HD:, :].rearrange("(j p) (f n) -> f p j n", p=HD, n=P)
                panel(slot, [(raw[:, slot, 0:CC], cols[f]), (raw[0:HD, slot, CC:DC], lo[f]),
                             (raw[HD:P, slot, CC:DC], hi[f])])

            for f in range(2):
                out_panel(f, f)
            sp.wait_ge(panel_split, T.last(panel_split) + 1)
            sp.wait_ge(conv_m, 3 + 3 * CC)
            for k in range(LATE):
                if k >= 4:
                    sp.wait_ge(mod_lo, k - 3)
                chunk = 2 * DC + k // 4 * 4
                src = io["mod_w"][chunk // (KINDS * DC)][256 * (k % 4):256 * (k % 4 + 1)]
                c0 = chunk % (KINDS * DC) * P
                sp.dma_start(mod_p[k % 4][:], src[:, c0:c0 + 512].rearrange("(k p) n -> p k n", p=P)).then_inc(
                    modp_landed[k % 4], 16)
            sp.wait_ge(mod_lo, LATE)
            for f in range(2, DC):
                out_panel(f % SLOTS, f)

            def mlp_panels(layer, s0):
                w1, w2 = io["mlp_w1"][layer], io["mlp_w2"][layer]
                rows = w2.rearrange("(f p) (k n) -> f p k n", p=P, n=P)
                for s in range(2):
                    panel((s0 + s) % SLOTS, [(raw[:, (s0 + s) % SLOTS], columns(w1, s))])
                with T.loop(sp, PAIRS - 1, [(panel_split, 4)]) as i:
                    for s in range(2):
                        slot = (s0 + 2 + s) % SLOTS
                        panel(slot, [(raw[:, slot], columns(w1, i * 2 + 2 + s))])
                    for s in range(2):
                        slot = (s0 + s) % SLOTS
                        panel(slot, [(raw[:, slot], rows[i * 2 + s])])
                for s in range(2):
                    slot = (s0 + 2 + s) % SLOTS
                    panel(slot, [(raw[:, slot], rows[2 * PAIRS - 2 + s])])

            mlp_panels(0, 0)
            if STAGE < 2:
                return
            gla = io["gla_w_in"][0]
            panel(0, [(raw[:, 0, :, 0:2 * RANK], gla[:, GLA_IN - 2 * RANK:].rearrange("(k p) n -> p k n", p=P))])
            for part in range(2):
                with T.loop(sp, 3, [(panel_split, 4)]) as i:
                    for s in range(4):
                        src = gla[:, 0:3 * D]
                        panel((1 + s) % SLOTS, [(raw[:, (1 + s) % SLOTS], columns(src, i * 4 + s + 12 * part))])
            sp.wait_ge(gla_free, 1)
            with T.loop(sp, 2, [(panel_split, 4)]) as i:
                for s in range(4):
                    panel((1 + s) % SLOTS, [(raw[:, (1 + s) % SLOTS], columns(io["gla_w_out"][0], i * 4 + s))])
            mlp_panels(1, 1)

        def terms():
            out = []
            for tile in [0] + list(range(TILES - 1, 0, -1)):
                if tile != 1:
                    out.append(("k", 1, tile, None))
                if tile:
                    out.append(("q", 1, tile, None))
            for tile in range(TILES):
                for level in range(len(LEVELS)):
                    out += [("pair", 0, tile, level), ("pair", 1, tile, level)]
                if tile:
                    out.append(("q", 0, tile, None))
                if tile < TILES - 1:
                    out.append(("k", 0, tile, None))
            return out

        def relative(kind, d):
            return kind == "pair" or (kind, d) in (("k", 0), ("q", 1))

        def halves(t, level):
            return t.rearrange("p h (b s n) -> p (h b) s n", s=2, n=LEVELS[level])

        def pool_gla(pool, T):
            pool.wait_ge(g_sum, 2)
            used = []
            for i, (kind, d, tile, level) in enumerate(terms()):
                if not relative(kind, d):
                    continue
                n = len(used)
                if len(used) >= 2:
                    pool.wait_ge(e_ready, used[-2] + 1)
                b = bc_b if d else bc_f
                if kind == "pair":
                    nn = LEVELS[level]
                    v = b[:, tile].rearrange("p h (b m) -> p (h b) m", m=2 * nn)
                    ref = v[:, :, nn:nn + 1] if d else v[:, :, nn - 1:nn]
                    out = dd[n % 2][:, :, :].rearrange("p h (b m) -> p (h b) m", m=2 * nn)
                    nc.gpsimd.tensor_tensor(out, v, ref.broadcast_to(v.shape), ALU.subtract).then_inc(d_ready, 1)
                else:
                    ref = tot_b[:, tile].unsqueeze(2) if d else b[:, tile, :, P - 1:P]
                    nc.gpsimd.tensor_tensor(dd[n % 2][:], b[:, tile], ref.broadcast_to([P, GH, P]),
                                            ALU.subtract).then_inc(d_ready, 1)
                used.append(i)

        @block.gpsimd
        def _(pool):
            T = Tally()
            nc.gpsimd.memset(one1[:], 1.0).then_inc(hi_split, 1)
            pool.wait_ge(hi_split, T.next(hi_split))
            pool.sem_inc(panel_split, 3)

            def split(slot, pieces=1, width=P):
                pool.wait_ge(raw_landed[slot], T.next(raw_landed[slot], 16 * pieces))
                pool.wait_ge(panel_used, T.next(panel_used))
                nc.gpsimd.tensor_tensor(w_hi[:, slot, :, 0:width], raw[:, slot, :, 0:width],
                                        one1[:].unsqueeze(1).broadcast_to([P, DC, width]), ALU.mult).then_inc(hi_split, 1)
                pool.wait_ge(hi_split, T.next(hi_split))
                nc.gpsimd.tensor_tensor(w_lo[:, slot, :, 0:width], raw[:, slot, :, 0:width],
                                        w_hi[:, slot, :, 0:width].bitcast(F32), ALU.subtract).then_inc(panel_split, 1)

            def per(*slots, pieces=1):
                return ([(raw_landed[s], 16 * pieces * slots.count(s)) for s in sorted(set(slots))]
                        + [(panel_used, len(slots)), (hi_split, len(slots))])

            with T.loop(pool, CC, per(0, 1, 2)):
                for s in range(3):
                    split(s)
            for s in range(2):
                split(s)
            for j in range(4):
                split((2 + j) % 3, pieces=2)
            for f in range(2):
                split(f, pieces=3)
            pool.wait_ge(csr_hi, 1)
            nc.gpsimd.tensor_tensor(csr[:, :, 2:4], csil[:], csr[:, :, 0:2].bitcast(F32), ALU.subtract)
            for k in range(LATE):
                pool.wait_ge(mod_hi, k + 1)
                nc.gpsimd.tensor_tensor(half_panel(w_lo, k), mod_p[k % 4][:], half_panel(w_hi, k).bitcast(F32),
                                        ALU.subtract).then_inc(mod_lo, 1)
            pool.wait_ge(modp_used, LATE)
            for f in range(2, DC):
                split(f % SLOTS, pieces=3)

            def scale_groups(t, first):
                for n in range(GROUPS):
                    pool.wait_ge(n_rc, first + n + 1)
                    nc.gpsimd.tensor_tensor(t[:, 3 * n:3 * n + 3], t[:, 3 * n:3 * n + 3],
                                            rts[n][:].unsqueeze(2).broadcast_to([P, GT, DC, P]), ALU.mult).then_inc(n_tm, 1)

            def mlp_splits(s0, t, first):
                split(s0)
                scale_groups(t, first)
                split(s0 + 1)
                with T.loop(pool, PAIRS - 1, per(0, 1, 2, 3)):
                    for s in (2, 3, 0, 1):
                        split((s0 + s) % SLOTS)
                for s in (2, 3):
                    split((s0 + s) % SLOTS)

            mlp_splits(0, t_b, 3)
            if STAGE < 2:
                scale_groups(t_b, 9)
                return
            split(0, width=2 * RANK)
            scale_groups(t_b, 9)
            for part in range(2):
                with T.loop(pool, 3, per(0, 1, 2, 3)):
                    for s in range(4):
                        split((1 + s) % SLOTS)
            pool_gla(pool, T)
            with T.loop(pool, 2, per(0, 1, 2, 3)):
                for s in range(4):
                    split((1 + s) % SLOTS)
            mlp_splits(1, t_a, 15)
            scale_groups(t_a, 21)

        @block.scalar
        def _(act):
            T = Tally()
            for b in range(3):
                act.sem_inc(unit_free[b], 1)
                T.add(unit_free[b])

            def take(out, bank, func=ACT.Copy, **kw):
                act.wait_ge(unit_ready[bank], T.next(unit_ready[bank]))
                nc.scalar.activation(out, ps[:, bank, 0:GN] if len(out.shape) == 2 else
                                     ps[:, bank, 0:GN].rearrange("p (t n) -> p t n", t=out.shape[1]),
                                     func, **kw).then_inc(unit_free[bank], 1)
                T.add(unit_free[bank])

            def own(ins):
                ins.then_inc(act_own, 1)
                act.wait_ge(act_own, T.next(act_own))

            act.wait_ge(vec_copied, 1)
            nc.scalar.activation(csil[:, :, :], vec1[:, 96:112].rearrange("p (c k) -> p k c", c=2),
                                 ACT.Silu).then_inc(csil_ready, 1)
            act.wait_ge(csil_ready, 1)
            nc.scalar.activation(csr[:, :, 0:2], csil[:], ACT.Copy).then_inc(csr_hi, 1)

            def square(dst, src):
                nc.scalar.activation(dst, src, ACT.Square).then_inc(n_sq, 1)

            def root(i):
                act.wait_ge(n_sum, T.next(n_sum))
                nc.scalar.activation(rts[i][:], ps[:, 7 - i % 2, 0:GN].rearrange("p (t n) -> p t n", t=GT), ACT.Sqrt,
                                     bias=eps[:, 0:1], scale=1.0 / D).then_inc(n_rt, 1)

            def affine(n, t, hi, layer, kind):
                act.wait_ge(n_xn, T.next(n_xn))
                for c in range(DC):
                    for lo, up, cond in ([(0, 1, 0), (1, 3, 1)] if n == 0 else [(0, 3, 1)]):
                        x = t[:, 3 * n + lo:3 * n + up, c, :]
                        last = nc.scalar.activation(x, x, ACT.Identity, bias=mods[:, layer, kind, c, cond:cond + 1],
                                                    scale=mods[:, layer, kind + 1, c, cond:cond + 1])
                last.then_inc(n_h, 1)
                act.wait_ge(n_h, T.next(n_h))
                nc.scalar.activation(hi[:, 3 * n:3 * n + 3], t[:, 3 * n:3 * n + 3], ACT.Copy).then_inc(n_hi, 1)

            def store_x(n):
                act.dma_start(x_d[3 * n:3 * n + 3].rearrange("t p m -> p t m"),
                              xb[n][:].rearrange("p t c n -> p t (c n)")).then_inc(x_stored, 16)
                T.add(x_stored, 16)

            def load_x(n):
                act.dma_start(xb[n][:].rearrange("p t c n -> p t (c n)"),
                              x_d[3 * n:3 * n + 3].rearrange("t p m -> p t m")).then_inc(x_loaded[n], 16)

            for n in range(GROUPS):
                for c in range(DC):
                    take(xb[n][:, :, c, :], (n * DC + c) % 3)
                for b in range(3):
                    act.wait_ge(unit_free[b], T.last(unit_free[b]))
                store_x(n)
                square(sq_c[:, 3 * n:3 * n + 3], xb[n][:])
            for n in range(GROUPS):
                root(n)
            act.wait_ge(mods_ready, 1)
            for n in range(GROUPS):
                affine(n, t_b, h_ac[0], 0, 0)
            T.n[n_lo.name] = GROUPS

            def both_norms(t, sq1, sq2, hi, layer, kind, before, final=False):
                def g(a, n):
                    return a[:, 3 * n:3 * n + 3]

                act.wait_ge(x_stored, T.last(x_stored))
                before(-1)
                load_x(0)
                for n in range(GROUPS):
                    before(n)
                    square(g(sq1, n), g(t, n))
                    if n == 1:
                        root(0)
                for n in (1, 2):
                    load_x(n)
                root(1)
                root(2)
                if not final:
                    for n in range(GROUPS):
                        act.wait_ge(n_x, T.next(n_x))
                        store_x(n)
                        square(g(sq2, n), xb[n][:])
                        if n:
                            root(2 + n)
                    affine(0, t, hi, layer, kind)
                    root(5)
                    for n in (1, 2):
                        affine(n, t, hi, layer, kind)
                    T.add(n_lo, 3)
                    return
                for n in range(GROUPS):
                    for c in range(DC):
                        take(y_sb[:, 3 * n:3 * n + 3, c * P:(c + 1) * P], (n * DC + c) % 3)
                    for b in range(3):
                        act.wait_ge(unit_free[b], T.last(unit_free[b]))
                    if n == 0:
                        act.dma_start(io["y_prompt"][0], y_sb[:, 0, :]).then_inc(y_out, 16)
                        act.dma_start(io["y_sample"][0, 0:256].rearrange("(t p) d -> p t d", p=P),
                                      y_sb[:, 1:3, :]).then_inc(y_out, 16)
                    else:
                        act.dma_start(io["y_sample"][0, GN * n - P:GN * (n + 1) - P].rearrange("(t p) d -> p t d", p=P),
                                      y_sb[:, 3 * n:3 * n + 3, :]).then_inc(y_out, 16)

            def taken(n):
                pass

            def summed(n):
                for b in range(4):
                    act.wait_ge(acc_free[b], acc[b] - (6 if n < 0 else 2 * (GROUPS - 1 - n)))

            per = [(unit_ready[b], 3) for b in range(3)] + [(unit_free[b], 3) for b in range(3)]
            with T.loop(act, CC, per + [(conv_m, 3), (conv_y, 1), (conv_u, 3)]):
                for n in range(GROUPS):
                    act.wait_ge(conv_m, T.next(conv_m))
                    take(c_cv[:, GN * n:GN * (n + 1)], n)
                act.wait_ge(conv_y, T.next(conv_y))
                act.wait_ge(u_clear, 1)
                for n in range(GROUPS):
                    act.wait_ge(unit_ready[n], T.next(unit_ready[n]))
                    if n == 0:
                        nc.scalar.activation(u_cv[:, 1:P + 1], ps[:, n, 0:P], ACT.Copy)
                        nc.scalar.activation(u_cv[:, P + 3:GN + 3], ps[:, n, P:GN], ACT.Copy).then_inc(unit_free[n], 1)
                    else:
                        nc.scalar.activation(u_cv[:, GN * n + 3:GN * (n + 1) + 3], ps[:, n, 0:GN],
                                             ACT.Copy).then_inc(unit_free[n], 1)
                    T.add(unit_free[n])
                for n in range(GROUPS):
                    act.wait_ge(conv_u, T.next(conv_u))
                    take(c_cv[:, GN * n:GN * (n + 1)], n)
            for dst, scale in [(k_t[:], 1.0), (v_t[:], 1.0)] + [(q_t[:, j, :], HD ** -0.5) for j in range(4)]:
                for n in range(GROUPS):
                    take(dst[:, GN * n:GN * (n + 1)], n, scale=scale)

            for b in range(3):
                act.wait_ge(unit_free[b], T.last(unit_free[b]))
            for dst, src in ((cosT[:], io["c_cos"]), (sinT[:], io["c_sin"]), (rot[:], io["c_rot"]), (band[:], io["c_band"]),
                             (kc_n[:], io["cache_k"][0, 0].rearrange("(t p) h d -> p t (h d)", p=P)),
                             (v_c[:], io["cache_v"][0, 0].rearrange("(t p) h d -> p t (h d)", p=P))):
                act.dma_start(dst, src).then_inc(att_in, 16)
            for n in range(GROUPS):
                take(v_n[:, 3 * n:3 * n + 3, :], n)
            act.wait_ge(unit_ready[0], T.next(unit_ready[0]))
            nc.scalar.activation(kc_t[:], ps[:, 0, 0:2 * P], ACT.Copy)
            nc.scalar.activation(k_out[:], ps[:, 0, 2 * P:3 * P], ACT.Copy).then_inc(unit_free[0], 1)
            T.add(unit_free[0])
            for b in range(3):
                act.wait_ge(unit_free[b], T.last(unit_free[b]))
            act.dma_start(io["new_cache_k"][0, 0].rearrange("s h d -> s (h d)"), k_out[:]).then_inc(cache_out, 16)
            act.dma_start(io["new_cache_v"][0, 0].rearrange("s h d -> s (h d)"), v_n[:, 0, :]).then_inc(cache_out, 16)

            def mod_split(k):
                act.wait_ge(modp_landed[k % 4], 16 * (k // 4 + 1))
                if k >= 2:
                    act.wait_ge(modp_used, k - 1)
                nc.scalar.activation(half_panel(w_hi, k), mod_p[k % 4][:], ACT.Copy).then_inc(mod_hi, 1)

            def mod_take(q):
                act.wait_ge(modp_used, 4 * q + 4)
                if q >= 2:
                    act.wait_ge(mod_turned, q - 1)
                nc.scalar.activation(mod_r[q % 2][:], ps[0:4, MOD_BANK, :], ACT.Copy).then_inc(mod_rows, 1)

            steps = attention_steps()
            for it in range(len(steps) + 4):
                if 3 <= it < len(steps) + 3:
                    b, j, u, tiles = steps[it - 3]
                    act.wait_ge(pt_ready, it - 2)
                    if it >= 5:
                        act.wait_ge(pv_ready, it - 4)
                    m = min(3, len(tiles))
                    nc.scalar.activation(prT[(it - 3) % 2][:, 0:m, :], ps[:, 0, 0:m * P].rearrange("p (t n) -> p t n", t=m),
                                         ACT.Copy).then_inc(pt_a, 1)
                if it >= 4 and steps[it - 4][2] == 1:
                    b, j, u, tiles = steps[it - 4]
                    act.wait_ge(pv_ready, it - 3)
                    nc.scalar.activation(at_hi[:, b, j, :], ps[:, O_BANK, 0:P], ACT.Copy).then_inc(ao_hi, 1)
                if it >= 5 and it % 4 == 1:
                    mod_take((it - 5) // 4)
                if it < len(steps):
                    b, j, u, tiles = steps[it]
                    x = smx[:, it % 3, :]
                    act.wait_ge(s_max, it + 1)
                    nc.scalar.activation(prob[it % 3][:, 0:len(tiles) * P], s_bank(it)[:, 0:len(tiles) * P], ACT.Exp,
                                         bias=x[:, 1:2], accum_out=x[:, 2:3])
                    head = j + 4 * u
                    nc.scalar.activation(x[:, 3:4], sink[:, head:head + 1], ACT.Exp, bias=x[:, 1:2]).then_inc(s_exp, 1)
                mod_split(it)
            for k in range(len(steps) + 4, LATE):
                mod_split(k)
                if k % 4 == 0:
                    mod_take(k // 4 - 1)
            mod_take(LATE // 4 - 1)

            def out_takes(t):
                per = [(unit_ready[b], 4) for b in range(3)] + [(unit_free[b], 4) for b in range(3)]
                with T.loop(act, 2, per) as i:
                    for s in range(4):
                        for n in range(GROUPS):
                            act.wait_ge(unit_ready[n], T.next(unit_ready[n]))
                            act.sem_inc(act_gate, 1)
                            nc.scalar.activation(t[:, 3 * n:3 * n + 3, bass.ds(i * 4 + s, 1), :],
                                                 ps[:, n, 0:GN].rearrange("p (t o n) -> p t o n", t=GT, o=1),
                                                 ACT.Copy).then_inc(unit_free[n], 1)
                            T.add(unit_free[n])
                for b in range(3):
                    act.wait_ge(unit_free[b], T.last(unit_free[b]))

            def mlp_hidden(p):
                for f in range(2):
                    for n in range(GROUPS):
                        x = relu[(f * 3 + n) % 2]
                        act.wait_ge(sq_done, T.next(sq_done))
                        take(x[:], n, ACT.Relu)
                        act.wait_ge(unit_free[n], T.last(unit_free[n]))
                        nc.scalar.activation(hidden[p][0][:, f, GN * n:GN * (n + 1)], x[:], ACT.Square).then_inc(hid_hi, 1)
                        T.add(hid_hi)

            def mlp():
                act.wait_ge(n_lo, T.last(n_lo))
                act.wait_ge(x_stored, T.last(x_stored))
                mlp_hidden(0)
                per = [(unit_ready[b], 4) for b in range(3)] + [(unit_free[b], 4) for b in range(3)]
                with T.loop(act, (PAIRS - 2) // 2, per + [(sq_done, 12), (hid_hi, 12)]):
                    for p in (1, 0):
                        mlp_hidden(p)
                mlp_hidden(1)
                for b in range(4):
                    acc[b] += PAIRS * 2 * GROUPS

            acc = [3, 3, 3, 3]
            for b, n in enumerate((3, 3, 2, 2)):
                acc[b] += n
            out_takes(t_b)
            act.wait_ge(cache_out, 32)
            both_norms(t_b, sq_a, sq_c, h_ac[0], 0, 3, taken)
            mlp()
            if STAGE < 2:
                both_norms(t_b, sq_a, None, None, 0, 0, summed, final=True)
                act.wait_ge(y_out, 64)
                act.wait_ge(cache_out, 32)
                return
            both_norms(t_b, sq_a, sq_c, h_ac[0], 1, 0, summed)

            for n in range(GROUPS):
                act.wait_ge(unit_ready[n], T.next(unit_ready[n]))
                nc.scalar.activation(r_t[:, GN * n:GN * (n + 1)], ps[0:2 * RANK, n, 0:GN], ACT.Copy).then_inc(unit_free[n], 1)
                T.add(unit_free[n])
            act.wait_ge(n_lo, T.last(n_lo))
            act.wait_ge(x_stored, T.last(x_stored))
            for dst, scale in ((gq, P ** -0.5), (gk, 1.0)):
                for h in range(GH):
                    for n in range(GROUPS):
                        take(dst[:, 3 * n:3 * n + 3, h, :], n, scale=scale)
            per = [(unit_ready[b], 4) for b in range(3)] + [(unit_free[b], 4) for b in range(3)]
            for b in range(4):
                T.n[acc_free[b].name] = acc[b]
            with T.loop(act, 2, per + [(acc_free[b], 3) for b in range(4)]):
                for u in range(12):
                    if u < 2:
                        act.wait_ge(acc_free[u + 2], T.last(acc_free[u + 2]))
                    else:
                        act.wait_ge(acc_free[(u - 2) % 4], T.next(acc_free[(u - 2) % 4]))
                    take(v_tmp[u % 2][:], u % 3)
                for b in (2, 3):
                    T.add(acc_free[b])
            act.wait_ge(acc_free[2], T.last(acc_free[2]))
            act.wait_ge(acc_free[3], T.last(acc_free[3]))
            for n in range(3):
                act.sem_inc(og_out[n], 16)
            og_rows = og_d.rearrange("t p (c n) -> c p t n", c=DC)
            with T.loop(act, 2, per + [(og_out[n], 64) for n in range(3)] + [(act_own, 12)]) as i:
                for s in range(4):
                    for n in range(GROUPS):
                        act.wait_ge(og_out[n], T.next(og_out[n], 16))
                        take(og_s[n][:], n, ACT.Silu)
                        act.wait_ge(unit_free[n], T.last(unit_free[n]))
                        own(nc.scalar.activation(og_s[n][:], og_s[n][:], ACT.Copy, scale=vec2[:, 72 + s % 2:73 + s % 2]))
                        act.dma_start(og_rows[i * 4 + s][:, 3 * n:3 * n + 3, :],
                                      og_s[n][:].rearrange("p (t n) -> p t n", t=GT)).then_inc(og_out[n], 16)

            for b in range(3):
                act.wait_ge(unit_free[b], T.last(unit_free[b]))
            act.wait_ge(dve_set, 4)
            for d in range(2):
                act.dma_start(gw[RANK * d:RANK * (d + 1), d, :], io["gla_gate_w"][0, d]).then_inc(gla_in, 16)
            for d in range(2):
                if d:
                    act.wait_ge(g_sum, 1)
                for u in range(12):
                    h, n = u // 3, u % 3
                    take(g_x[:, u, :], n, ACT.Identity, bias=vec2[:, 64 + 4 * d + h:65 + 4 * d + h])
                act.wait_ge(g_neg, d + 1)
                own(nc.scalar.activation(g_l[:], g_l[:], ACT.Exp))
                nc.scalar.activation(g_l[:], g_l[:], ACT.Ln, bias=1.0).then_inc(g_ln, 1)
            act.wait_ge(g_sum, 2)
            act.dma_start(masks[:], io["c_masks"]).then_inc(mask_in, 16)
            nc.scalar.activation(dec[:, 0:TILES, :], bc_f[:, :, :, P - 1], ACT.Exp, scale=1 / GATE_NORM)
            nc.scalar.activation(dec[:, TILES:2 * TILES, :], tot_b[:], ACT.Exp, scale=1 / GATE_NORM).then_inc(dec_ready, 1)

            order = terms()
            state = {"rel": 0, "upd": 0, "ob": 0}

            def exp_term(i):
                kind, d, tile, level = order[i]
                e = ee[i % 2]
                if i >= 2:
                    act.wait_ge(xt_ready, i - 1)
                if relative(kind, d):
                    state["rel"] += 1
                    act.wait_ge(d_ready, state["rel"])
                    x = dd[(state["rel"] - 1) % 2]
                if kind == "pair":
                    a, b = halves(x[:], level), halves(e[:], level)
                    nc.scalar.activation(b[:, :, 0, :], a[:, :, 0, :], ACT.Exp, scale=-1 / GATE_NORM)
                    nc.scalar.activation(b[:, :, 1, :], a[:, :, 1, :], ACT.Exp, scale=1 / GATE_NORM).then_inc(e_ready, 1)
                elif relative(kind, d):
                    nc.scalar.activation(e[:], x[:], ACT.Exp, scale=-1 / GATE_NORM).then_inc(e_ready, 1)
                else:
                    nc.scalar.activation(e[:], (bc_b if d else bc_f)[:, tile], ACT.Exp, scale=1 / GATE_NORM).then_inc(e_ready, 1)

            def turn_k():
                state["upd"] += 1
                act.wait_ge(khn_t, state["upd"])
                if state["upd"] > 1:
                    act.wait_ge(upd_ready, state["upd"] - 1)
                nc.scalar.activation(khn[:].rearrange("p h n -> p (h n)"), ps[:, 2, :], ACT.Copy).then_inc(khn_ready, 1)

            def swap_state(count, dst, src):
                act.wait_ge(st_ready, count)
                act.dma_start(dst[0, 0].rearrange("h k v -> k h v"), st[:]).then_inc(st_out, 16)
                act.wait_ge(st_out, 16 if dst is io["new_state_bwd"] else 32)
                act.dma_start(st[:], src[0, 0].rearrange("h k v -> k h v")).then_inc(st_in, 16)

            i = 0
            exp_term(0)
            i = 1
            turn_k()
            swap_state(1, io["new_state_bwd"], io["state_bwd"])
            for tile in range(TILES - 1, 0, -1):
                if tile != 1:
                    exp_term(i)
                    i += 1
                exp_term(i)
                i += 1
                if tile != 1:
                    turn_k()
                state["ob"] += 1
                act.wait_ge(ob_ready, state["ob"])
                nc.scalar.activation(o_b[:, tile, :], psf[:, 3 * 512:5 * 512], ACT.Copy).then_inc(ob_taken, 1)

            def load_og(tile):
                if tile >= 2:
                    act.wait_ge(ot_taken, 2 * (tile - 1))
                act.dma_start(og[tile % 2][:].rearrange("p c n -> p (c n)"), og_d[tile]).then_inc(og_in[tile % 2], 16)

            def head_norm(tile):
                act.wait_ge(o_sum, tile + 1)
                for h in range(GH):
                    own(nc.scalar.activation(junk[:], oo[:, h * DV:(h + 1) * DV], ACT.Square, accum_out=rs4[:, 0, h:h + 1]))
                nc.scalar.activation(rs4[:, 1, :], rs4[:, 0, :], ACT.Sqrt, bias=eps[:, 0:1], scale=1.0 / DV).then_inc(o_sq, 1)

            def gated_hi(tile):
                act.wait_ge(ot_taken, 2 * (tile + 1))
                nc.scalar.activation(m_hi[:, tile], mm_[:], ACT.Copy).then_inc(gm_hi, 1)

            for n in range(3):
                act.wait_ge(og_out[n], T.next(og_out[n], 16))
            for tile in range(TILES):
                if tile < 2:
                    load_og(tile)
                if tile >= 2:
                    act.wait_ge(o_ready, tile - 1)
                act.wait_ge(gram_ready, 15 * tile + 1)
                nc.scalar.activation(att[tile % 2][:].rearrange("p h n -> p (h n)"), ps[:, (15 * tile) % 2, :], ACT.Copy,
                                     scale=2.0).then_inc(diag_ready, 1)
                for j in range(14):
                    exp_term(i)
                    i += 1
                    if tile and j == 1:
                        head_norm(tile - 1)
                    if tile and j == 8:
                        gated_hi(tile - 1)
                        if tile + 1 < TILES:
                            load_og(tile + 1) if tile + 1 >= 2 else None
                if tile:
                    exp_term(i)
                    i += 1
                if tile < TILES - 1:
                    exp_term(i)
                    i += 1
                    turn_k()
                if tile == 0:
                    swap_state(9, io["new_state_fwd"], io["state_fwd"])
            head_norm(TILES - 1)
            gated_hi(TILES - 1)
            act.wait_ge(gm_lo, TILES)
            act.sem_inc(gla_free, 1)

            out_takes(t_a)
            both_norms(t_a, sq_b, sq_c, h_bc[0], 1, 3, taken)
            for b in range(4):
                acc[b] = T.last(acc_free[b])
            mlp()
            both_norms(t_a, sq_b, None, None, 1, 0, summed, final=True)
            act.wait_ge(y_out, 64)
            act.wait_ge(cache_out, 32)
            act.wait_ge(st_out, 32)

        @block.vector
        def _(dve):
            T = Tally()
            V = nc.vector

            def own(ins):
                ins.then_inc(dve_own, 1)
                dve.wait_ge(dve_own, T.next(dve_own))

            V.memset(ones[:], 1.0).then_inc(dve_set, 1)
            V.memset(eps[:], EPS).then_inc(dve_set, 1)
            dve.wait_ge(hi_split, 1)
            for b in range(4):
                dve.sem_inc(acc_free[b], 1)
                T.add(acc_free[b])
            dve.sem_inc(sq_done, 2)
            T.add(sq_done, 2)
            dve.sem_inc(conv_m, 3)
            dve.sem_inc(conv_y, 1)
            T.add(conv_m, 3)
            T.add(conv_y, 1)

            def full(t, n):
                return t[:, 3 * n:3 * n + 3]

            dve.wait_ge(vec_turned, 1)
            V.tensor_copy(vec1[:, 0:124], ps[:, 7, 0:124]).then_inc(vec_copied, 1)
            V.tensor_copy(vec2[:, 0:74], ps[:, 7, P:P + 74]).then_inc(vec_copied, 1)
            dve.wait_ge(vec_copied, 2)
            for layer in range(2):
                bias = vec1[:, 48 * layer:48 * (layer + 1)].rearrange("p (a c) -> p a c", c=DC).unsqueeze(3)
                last = V.tensor_copy(mods[:, layer], bias.broadcast_to([P, KINDS, DC, 2]))
            own(last)
            m0 = mods[:, 0, 0:2].rearrange("p a c k -> p (a c k)")
            with T.loop(dve, 2, [(acc_ready[b], 1) for b in range(4)] + [(acc_free[b], 1) for b in range(4)]):
                for b in range(4):
                    dve.wait_ge(acc_ready[b], T.next(acc_ready[b]))
                    dve.wait_ge(acc_free[b - 1], T.last(acc_free[b - 1]))
                    V.tensor_tensor(m0, ps[:, 3 + b, 0:32], m0, ALU.add).then_inc(acc_free[b], 1)
                    T.add(acc_free[b])
            dve.wait_ge(acc_free[3], T.last(acc_free[3]))

            def weigh(layer, kind, norm, plus):
                g = vec2[:, 32 * layer + 8 * norm:32 * layer + 8 * (norm + 1)].unsqueeze(2).broadcast_to([P, DC, 2])
                return V.scalar_tensor_tensor(out=mods[:, layer, kind], in0=mods[:, layer, kind], scalar=plus, in1=g,
                                              op0=ALU.add, op1=ALU.mult)

            weigh(0, 1, 0, 1.0).then_inc(mods_ready, 1)

            def g3(t, n):
                return t[:, 3 * n:3 * n + 3]

            def inverse(i):
                dve.wait_ge(n_rt, T.next(n_rt))
                V.reciprocal(rts[i][:], rts[i][:]).then_inc(n_rc, 1)
                T.add(n_rc)

            def normed(n, t, i):
                dve.wait_ge(n_rc, T.last(n_rc))
                V.tensor_tensor(g3(t, n), xb[n][:], rts[i][:].unsqueeze(2).broadcast_to([P, GT, DC, P]),
                                ALU.mult).then_inc(n_xn, 1)

            def low(n, t, h):
                dve.wait_ge(n_hi, T.next(n_hi))
                V.tensor_tensor(g3(h[1], n), g3(t, n), g3(h[0], n).bitcast(F32), ALU.subtract).then_inc(n_lo, 1)
                T.add(n_lo)

            for n in range(GROUPS):
                inverse(n)
                normed(n, t_b, n)
            for n in range(GROUPS):
                low(n, t_b, h_ac)

            def both_norms(t, h, layer, gate, clear=False, final=False):
                def residual(n):
                    dve.wait_ge(n_tm, T.next(n_tm))
                    dve.wait_ge(x_loaded[n], T.next(x_loaded[n], 16))
                    for c in range(DC):
                        for lo, up, cond in ([(0, 1, 0), (1, 3, 1)] if n == 0 else [(0, 3, 1)]):
                            last = V.scalar_tensor_tensor(out=xb[n][:, lo:up, c, :], in0=t[:, 3 * n + lo:3 * n + up, c, :],
                                                          scalar=mods[:, layer, gate, c, cond:cond + 1],
                                                          in1=xb[n][:, lo:up, c, :], op0=ALU.mult, op1=ALU.add)
                    last.then_inc(n_x, 1)
                    T.add(n_x)

                inverse(0)
                inverse(1)
                residual(0)
                inverse(2)
                residual(1)
                residual(2)
                if final:
                    return
                dve.wait_ge(n_x, T.last(n_x))
                inverse(3)
                normed(0, t, 3)
                inverse(4)
                normed(1, t, 4)
                low(0, t, h)
                inverse(5)
                normed(2, t, 5)
                low(1, t, h)
                low(2, t, h)
                if clear:
                    dve.wait_ge(n_lo, T.last(n_lo))
                    own(V.memset(t[:], 0.0))

            dve.wait_ge(x_stored, 16 * GROUPS)
            V.memset(u_cv[:], 0.0).then_inc(u_clear, 1)
            dve.wait_ge(u_clear, 1)
            for b in range(3):
                T.add(unit_free[b], 1 + 8)
            per = [(unit_free[b], 3) for b in range(3)] + [(conv_u, 3), (conv_y, 1), (conv_m, 3), (dve_own, 9)]
            with T.loop(dve, CC, per) as i:
                dve.wait_ge(conv_y, T.last(conv_y))
                own(V.tensor_tensor(cw[:].unsqueeze(2), vec1[:, 112:124].rearrange("p (w c) -> p w c", w=3)[:, :, bass.ds(i, 1)],
                                    one1[:].unsqueeze(1).broadcast_to([P, 3, 1]), ALU.mult))
                for n in range(GROUPS):
                    dve.wait_ge(unit_free[n], T.next(unit_free[n], 2))
                    for d0, s0, m in ([(1, 0, P), (P + 3, P, GN - P)] if n == 0 else [(GN * n + 3, GN * n, GN)]):
                        last = V.tensor_tensor(u_cv[:, d0:d0 + m], u_cv[:, d0:d0 + m], c_cv[:, s0:s0 + m], ALU.mult)
                    last.then_inc(conv_u, 1)
                    T.add(conv_u)
                dve.wait_ge(conv_u, T.last(conv_u))
                own(V.tensor_scalar(y_cv[:], u_cv[:, 0:1154], cw[:, 0:1], None, ALU.mult))
                own(V.scalar_tensor_tensor(out=y_cv[:], in0=u_cv[:, 1:1155], scalar=cw[:, 1:2], in1=y_cv[:],
                                           op0=ALU.mult, op1=ALU.add))
                V.scalar_tensor_tensor(out=y_cv[:], in0=u_cv[:, 2:1156], scalar=cw[:, 2:3], in1=y_cv[:],
                                       op0=ALU.mult, op1=ALU.add).then_inc(conv_y, 1)
                dve.wait_ge(conv_y, T.next(conv_y))
                for n in range(GROUPS):
                    dve.wait_ge(unit_free[n], T.next(unit_free[n]))
                    m = m_f[n % 2]
                    dve.wait_ge(conv_m, T.last(conv_m))
                    if n == 0:
                        V.tensor_tensor(m[:, 0:P], y_cv[:, 0:P], c_cv[:, 0:P], ALU.mult)
                        own(V.tensor_tensor(m[:, P:GN], y_cv[:, P + 2:GN + 2], c_cv[:, P:GN], ALU.mult))
                    else:
                        own(V.tensor_tensor(m[:], y_cv[:, GN * n + 2:GN * (n + 1) + 2], c_cv[:, GN * n:GN * (n + 1)], ALU.mult))
                    v = m[:].rearrange("p (t o n) -> p t o n", t=GT, o=1)
                    hi = conv_hi[:, 3 * n:3 * n + 3, bass.ds(i, 1), :]
                    own(V.tensor_tensor(hi, v, one1[:].unsqueeze(2).unsqueeze(3).broadcast_to([P, GT, 1, P]), ALU.mult))
                    V.tensor_tensor(conv_lo[:, 3 * n:3 * n + 3, bass.ds(i, 1), :], v, hi.bitcast(F32),
                                    ALU.subtract).then_inc(conv_m, 1)
                    T.add(conv_m)
            dve.wait_ge(conv_m, T.last(conv_m))

            dve.wait_ge(att_in, 96)
            r = 0
            for t in [k_t[:]] + [q_t[:, j, :] for j in range(4)]:
                for half in range(2):
                    b = r % 4
                    dve.wait_ge(acc_ready[b], T.next(acc_ready[b]))
                    x = t[:, P + 512 * half:P + 512 * (half + 1)]
                    a = slice(512 * half, 512 * (half + 1))
                    V.tensor_tensor(rt2[:], ps[:, 3 + b, :], sinT[:, a], ALU.mult).then_inc(acc_free[b], 1)
                    own(V.tensor_tensor(rt1[:], x, cosT[:, a], ALU.mult))
                    dve.wait_ge(acc_free[b], T.next(acc_free[b]))
                    V.tensor_tensor(x, rt1[:], rt2[:], ALU.add).then_inc(rope_done, 1)
                    r += 1
                    dve.wait_ge(rope_done, r)

            late = mods[:].rearrange("p l a c k -> p (l a c) k")[:, 2 * DC:]

            def mod_add(q):
                dve.wait_ge(mod_turned, q + 1)
                turned = ps[:, 1, 256:272].rearrange("p (c k) -> p c k", k=4)
                m = late[:, 4 * q:4 * q + 4]
                own(V.tensor_tensor(m, turned[:, :, 0:2], m, ALU.add))
                V.tensor_tensor(m, turned[:, :, 2:4], m, ALU.add).then_inc(mod_added, 1)

            steps = attention_steps()
            wide = 0
            for it in range(len(steps) + 4):
                if 3 <= it < len(steps) + 3:
                    b, j, u, tiles = steps[it - 3]
                    if len(tiles) > 3:
                        dve.wait_ge(pt_ready, it - 2)
                        if it >= 5:
                            dve.wait_ge(pv_ready, it - 4)
                        m = len(tiles) - 3
                        V.tensor_copy(prT[(it - 3) % 2][:, 3:3 + m, :],
                                      ps[:, 1, 0:m * P].rearrange("p (t n) -> p t n", t=m)).then_inc(pt_v, 1)
                if it >= 4 and steps[it - 4][2] == 1:
                    b, j, u, tiles = steps[it - 4]
                    dve.wait_ge(ao_hi, (it - 4) // 2 + 1)
                    V.tensor_tensor(at_lo[:, b, j, :], ps[:, O_BANK, 0:P], at_hi[:, b, j, :].bitcast(F32),
                                    ALU.subtract).then_inc(ao_lo, 1)
                if it >= 7 and it % 4 == 3:
                    dve.wait_ge(pt_ready, min(it - 2, len(steps)))
                    mod_add((it - 7) // 4)
                if 1 <= it <= len(steps):
                    b, j, u, tiles = steps[it - 1]
                    x = smx[:, (it - 1) % 3, :]
                    dve.wait_ge(s_exp, it)
                    own(V.tensor_tensor(x[:, 4:5], x[:, 2:3], x[:, 3:4], ALU.add))
                    own(V.reciprocal(x[:, 5:6], x[:, 4:5]))
                    pr = prob[(it - 1) % 3][:, 0:len(tiles) * P]
                    V.tensor_scalar(pr, pr, x[:, 5:6], None, ALU.mult).then_inc(s_norm, 1)
                if it < len(steps):
                    b, j, u, tiles = steps[it]
                    x = smx[:, it % 3, :]
                    s = s_bank(it)
                    dve.wait_ge(s_ready, it + 1)
                    last = None
                    for pos, (what, tile) in enumerate(tiles):
                        if what == "own" and b and tile != b:
                            cols = s[:, pos * P:(pos + 1) * P]
                            last = V.tensor_tensor(cols, cols, band[:, 0 if tile < b else 1, :], ALU.add)
                    if last is not None:
                        own(last)
                    own(V.tensor_reduce(x[:, 0:1], s[:, 0:len(tiles) * P], AX_X, ALU.max))
                    head = j + 4 * u
                    V.tensor_scalar(x[:, 1:2], x[:, 0:1], sink[:, head:head + 1], -1.0, ALU.max, ALU.mult).then_inc(s_max, 1)

            for q in range(LATE // 4 - 2, LATE // 4):
                mod_add(q)
            dve.wait_ge(mod_added, LATE // 4)
            for layer in range(2):
                for kind, norm, plus in ((1, 0, 1.0), (2, 1, 0.0), (4, 2, 1.0), (5, 3, 0.0)):
                    if layer or kind > 1:
                        last = weigh(layer, kind, norm, plus)
            last.then_inc(mods_ready, 1)
            dve.wait_ge(mods_ready, 2)

            both_norms(t_b, h_ac, 0, 2, clear=True)

            def mlp_hidden(p):
                for f in range(2):
                    for n in range(GROUPS):
                        u = (f * 3 + n) % 2
                        dve.wait_ge(unit_free[n], T.next(unit_free[n]))
                        if T.n.get(hid_lo.name):
                            dve.wait_ge(hid_lo, T.last(hid_lo))
                        V.tensor_tensor(sqr[u][:], relu[u][:], relu[u][:], ALU.mult).then_inc(sq_done, 1)
                        dve.wait_ge(sq_done, T.next(sq_done))
                        dve.wait_ge(hid_hi, T.next(hid_hi))
                        V.tensor_tensor(hidden[p][1][:, f, GN * n:GN * (n + 1)], sqr[u][:],
                                        hidden[p][0][:, f, GN * n:GN * (n + 1)].bitcast(F32),
                                        ALU.subtract).then_inc(hid_lo, 1)
                        T.add(hid_lo)

            def mlp_sum(t):
                for n in range(GROUPS):
                    for c in range(DC):
                        b = c % 4
                        dve.wait_ge(acc_ready[b], T.next(acc_ready[b]))
                        x = t[:, 3 * n:3 * n + 3, c, :]
                        V.tensor_tensor(x, ps[:, 3 + b, 0:GN].rearrange("p (t n) -> p t n", t=GT), x,
                                        ALU.add).then_inc(acc_free[b], 1)
                        T.add(acc_free[b])

            def mlp(t):
                dve.wait_ge(n_lo, T.last(n_lo))
                mlp_hidden(0)
                per = [(unit_free[b], 4) for b in range(3)] + [(sq_done, 12), (hid_hi, 12), (hid_lo, 12)]
                per += [(acc_ready[b], 12) for b in range(4)] + [(acc_free[b], 12) for b in range(4)]
                with T.loop(dve, (PAIRS - 2) // 2, per):
                    for p in (1, 0):
                        mlp_hidden(p)
                        mlp_sum(t)
                mlp_hidden(1)
                mlp_sum(t)
                mlp_sum(t)
                for b in range(4):
                    dve.wait_ge(acc_free[b], T.last(acc_free[b]))

            for b, turned in enumerate((2, 1, 1)):
                T.add(unit_free[b], 6 + turned + 8)
            mlp(t_b)
            if STAGE < 2:
                both_norms(t_b, None, 0, 5, final=True)
                return
            both_norms(t_b, h_ac, 0, 5)

            with T.loop(dve, 2, [(acc_ready[b], 3) for b in range(4)] + [(acc_free[b], 3) for b in range(4)]) as i:
                for u in range(12):
                    b, n = u % 4, u % 3
                    dve.wait_ge(acc_ready[b], T.next(acc_ready[b]))
                    V.tensor_scalar(gv[:, 3 * n:3 * n + 3, bass.ds(i * 512 + (u // 3) * P, P)],
                                    ps[:, 3 + b, 0:GN].rearrange("p (t n) -> p t n", t=GT), 1.0, None,
                                    ALU.mult).then_inc(acc_free[b], 1)
                    T.add(acc_free[b])

            for b in range(3):
                dve.wait_ge(unit_free[b], T.next(unit_free[b], 1 + 8 + 8 + 8))
            V.memset(gw[:], 0.0).then_inc(dve_set, 1)
            V.memset(bc_b[:, :, :, 0:1], 0.0).then_inc(dve_set, 1)
            dve.wait_ge(dve_set, 4)
            for d in range(2):
                for b in range(3):
                    dve.wait_ge(unit_free[b], T.next(unit_free[b], 4))
                V.scalar_tensor_tensor(out=g_l[:], in0=g_x[:], scalar=-1.0, in1=g_x[:], op0=ALU.mult,
                                       op1=ALU.min).then_inc(g_neg, 1)
                dve.wait_ge(g_ln, d + 1)
                own(V.scalar_tensor_tensor(out=g_x[:], in0=g_x[:], scalar=0.0, in1=g_l[:], op0=ALU.min, op1=ALU.subtract))
                for h in range(GH):
                    for tile in range(TILES):
                        g = g_x[:, 3 * h + tile // GT, (tile % GT) * P:(tile % GT + 1) * P]
                        if d == 0:
                            last = V.tensor_tensor_scan(bc_f[:, tile, h, :], ones[:], g, 0.0, ALU.mult, ALU.add)
                        else:
                            last = V.tensor_tensor_scan(bc_b[:, tile, h, 1:P], ones[:, 0:P - 1], g[:, 0:P - 1], 0.0,
                                                        ALU.mult, ALU.add)
                if d:
                    own(last)
                    for h in range(GH):
                        g = g_x[:, 3 * h:3 * h + 3, :].rearrange("p u (t n) -> p (u t) n", n=P)
                        last = V.tensor_tensor(tot_b[:, :, h:h + 1], bc_b[:, :, h, P - 1:P], g[:, :, P - 1:P], ALU.add)
                last.then_inc(g_sum, 1)
            dve.wait_ge(g_sum, 2)
            for b in range(3):
                T.add(unit_free[b], -8)
            for b in range(3):
                T.add(unit_free[b], 8)

            order = terms()
            count = {"pair": 0, "st": 0, "upd": 0}

            def term(i):
                kind, d, tile, level = order[i]
                e = ee[i % 2]
                dve.wait_ge(e_ready, i + 1)
                if kind == "pair":
                    j = count["pair"]
                    count["pair"] += 1
                    if j >= 2:
                        k = j - 2
                        dve.wait_ge(gram_ready, 15 * (k // 14) + 2 + k % 14)
                    x = halves(xx[j % 2][:], level)
                    a, b = (gq, gk) if d else (gk, gq)
                    V.tensor_tensor(x[:, :, 0, :], halves(a[:, tile], level)[:, :, 0, :], halves(e[:], level)[:, :, 0, :], ALU.mult)
                    V.tensor_tensor(x[:, :, 1, :], halves(b[:, tile], level)[:, :, 1, :], halves(e[:], level)[:, :, 1, :],
                                    ALU.mult).then_inc(xt_ready, 1)
                else:
                    if kind == "k" and count["upd"]:
                        dve.wait_ge(khn_t, count["upd"])
                    if kind == "k":
                        count["upd"] += 1
                    if kind == "q":
                        if d and tile < TILES - 1:
                            dve.wait_ge(ob_ready, TILES - 1 - tile)
                        elif not d and tile > 1:
                            dve.wait_ge(o_ready, tile)
                        elif not d:
                            dve.wait_ge(ob_ready, TILES - 1)
                    V.tensor_tensor((kh if kind == "k" else qh)[:], (gk if kind == "k" else gq)[:, tile], e[:],
                                    ALU.mult).then_inc(xt_ready, 1)

            def update(d, tile):
                count["st"] += 1
                dve.wait_ge(upd_ready, count["st"])
                if tile == 0:
                    V.tensor_copy(st[:].rearrange("p h v -> p (h v)"), psf[:, 5 * 512:7 * 512]).then_inc(st_ready, 1)
                else:
                    for h in range(GH):
                        last = V.scalar_tensor_tensor(out=st[:, h, :], in0=st[:, h, :],
                                                      scalar=dec[:, TILES * d + tile, h:h + 1],
                                                      in1=psf[:, 5 * 512 + DV * h:5 * 512 + DV * (h + 1)],
                                                      op0=ALU.mult, op1=ALU.add)
                    last.then_inc(st_ready, 1)
                dve.wait_ge(st_ready, count["st"])

            dve.wait_ge(dec_ready, 1)
            i = 0
            for tile in [0] + list(range(TILES - 1, 0, -1)):
                for _ in range((tile != 1) + (tile != 0)):
                    term(i)
                    i += 1
                if tile == TILES - 1:
                    dve.wait_ge(st_in, 16)
                if tile != 1:
                    update(1, tile)

            def head_scale(tile):
                dve.wait_ge(o_sq, tile + 1)
                own(V.reciprocal(rs4[:, 1, :], rs4[:, 1, :]))
                o3 = oo[:].rearrange("p (h v) -> p h v", h=GH)
                V.tensor_tensor(o3, o3, rs4[:, 1, :].unsqueeze(2).broadcast_to([P, GH, DV]), ALU.mult).then_inc(o_nrm, 1)

            def gate_half(tile, half):
                dve.wait_ge(ot_ready, 2 * tile + half + 1)
                if half == 0:
                    dve.wait_ge(og_in[tile % 2], 16 * (tile // 2 + 1))
                    if tile:
                        dve.wait_ge(gm_lo, tile)
                V.tensor_tensor(mm_[:, 4 * half:4 * half + 4, :], ps[:, 7, :].rearrange("p (c n) -> p c n", c=4),
                                og[tile % 2][:, 4 * half:4 * half + 4, :], ALU.mult).then_inc(ot_taken, 1)

            def gated_lo(tile):
                dve.wait_ge(gm_hi, tile + 1)
                V.tensor_tensor(m_lo[:, tile], mm_[:], m_hi[:, tile].bitcast(F32), ALU.subtract).then_inc(gm_lo, 1)

            def place(tile, jj):
                dve.wait_ge(gram_ready, 15 * tile + 2 + jj)
                if jj == 0:
                    dve.wait_ge(diag_ready, tile + 1)
                    dve.wait_ge(mask_in, 16)
                else:
                    dve.wait_ge(gram_taken, 14 * tile + jj)
                level, d = jj // 2, jj % 2
                V.copy_predicated(att[tile % 2][:], masks[:, 2 * level + d, :].bitcast(mybir.dt.int32).unsqueeze(1).broadcast_to([P, GH, P]),
                                  ps[:, (15 * tile + 1 + jj) % 2, :].rearrange("p (h n) -> p h n", h=GH)).then_inc(gram_taken, 1)

            for tile in range(TILES):
                for j in range(14):
                    term(i)
                    i += 1
                    if j:
                        place(tile, j - 1)
                    if tile:
                        if j == 3:
                            head_scale(tile - 1)
                        if j == 5:
                            gate_half(tile - 1, 0)
                        if j == 7:
                            gate_half(tile - 1, 1)
                        if j == 10:
                            gated_lo(tile - 1)
                if tile:
                    term(i)
                    i += 1
                if tile < TILES - 1:
                    term(i)
                    i += 1
                place(tile, 13)
                dve.wait_ge(o_ready, tile + 1)
                if tile:
                    dve.wait_ge(ot_ready, 2 * tile)
                    V.tensor_tensor(oo[:], psf[:, 3 * 512:5 * 512], o_b[:, tile, :], ALU.add).then_inc(o_sum, 1)
                else:
                    V.tensor_copy(oo[:], psf[:, 3 * 512:5 * 512]).then_inc(o_sum, 1)
                if tile == 1:
                    dve.wait_ge(st_in, 32)
                if tile < TILES - 1:
                    update(0, tile)
            head_scale(TILES - 1)
            gate_half(TILES - 1, 0)
            gate_half(TILES - 1, 1)
            gated_lo(TILES - 1)

            both_norms(t_a, h_bc, 1, 2, clear=True)
            for b in range(3):
                T.add(unit_free[b], 8)
            mlp(t_a)
            both_norms(t_a, None, 1, 5, final=True)

        @block.tensor
        def _(pe):
            T = Tally()
            M = nc.tensor
            owed = [1]
            T.add(panel_split, 3)
            pe.sem_inc(panel_used, 2)


            def turn(out, in_):
                n = in_.shape[0]
                return M.transpose(out, in_, ident[0:n, 0:n])

            pe.wait_ge(const_in, 16 * N_CONST)
            turn(ps[:, 7, 0:124], rows1[0:124, :])
            turn(ps[:, 7, P:P + 74], rows2[0:74, :]).then_inc(vec_turned, 1)
            pe.wait_ge(csil_ready, 1)
            def first_mods():
                per = [(mod_landed[b], 16) for b in range(4)] + [(acc_free[b], 1) for b in range(4)]
                with T.loop(pe, 2, per) as i:
                    for b in range(4):
                        pe.wait_ge(mod_landed[b], T.next(mod_landed[b], 16))
                        pe.wait_ge(acc_free[b], T.next(acc_free[b]))
                        for f in range(2 * DC):
                            last = M.matmul(ps[:, 3 + b, 2 * f:2 * f + 2], mod_w[b][:, f * P:(f + 1) * P],
                                            csil[:, bass.ds(i * 4 + b, 1), :].rearrange("p o k -> p (o k)"),
                                            start=True, stop=True)
                        last.then_inc(acc_ready[b], 1)

            def late_mod(k):
                if k % 4 == 0 and k:
                    pe.wait_ge(mod_rows, k // 4)
                pe.wait_ge(mod_lo, k + 1)
                for w in (w_hi, w_lo):
                    for a in range(2):
                        last = M.matmul(ps[0:4, MOD_BANK, :], csr[:, 2 * (k % 4) + a, :], half_panel(w, k)[:, a, :],
                                        start=(k % 4 == 0 and a == 0 and w is w_hi),
                                        stop=(k % 4 == 3 and a == 1 and w is w_lo))
                last.then_inc(modp_used, 1)

            def mod_turn(q):
                pe.wait_ge(mod_rows, q + 1)
                if q:
                    pe.wait_ge(mod_added, q)
                for f in range(4):
                    last = turn(ps[:, 1, 256 + 4 * f:260 + 4 * f], mod_r[q % 2][:, f * P:(f + 1) * P])
                last.then_inc(mod_turned, 1)

            def norm_sum(sq, n, i):
                pe.wait_ge(n_sq, T.next(n_sq))
                if i >= 2:
                    pe.wait_ge(n_rt, T.last(n_rt) + i - 1)
                for c in range(DC):
                    last = M.matmul(ps[:, 7 - i % 2, 0:GN], ones[:], sq[:, 3 * n:3 * n + 3, c, :],
                                    start=(c == 0), stop=(c == DC - 1))
                last.then_inc(n_sum, 1)

            pe.wait_ge(dve_set, 1)
            for n in range(GROUPS):
                for c in range(DC):
                    bank = (n * DC + c) % 3
                    pe.wait_ge(unit_free[bank], T.next(unit_free[bank]))
                    for t in range(GT):
                        last = turn(ps[:, bank, t * P:(t + 1) * P], x_in[:, 3 * n + t, c * P:(c + 1) * P])
                    last.then_inc(unit_ready[bank], 1)
            first_mods()
            pe.wait_ge(vec_copied, 2)
            for b in range(4):
                pe.wait_ge(acc_free[b], T.last(acc_free[b]) + 1)
            for n in range(GROUPS):
                norm_sum(sq_c, n, n)
            pe.wait_ge(n_rt, T.next(n_rt, 3))

            def both_norms(sq1, sq2, final=False):
                for n in range(GROUPS):
                    if n == 1:
                        pe.wait_ge(acc_free[3], T.last(acc_free[3]) + 1)
                    norm_sum(sq1, n, n)
                if not final:
                    for n in range(GROUPS):
                        norm_sum(sq2, n, 3 + n)
                    T.add(n_x, 3)
                    pe.wait_ge(n_rt, T.next(n_rt, 6))
                    return
                for n in range(GROUPS):
                    pe.wait_ge(n_x, T.next(n_x))
                    for c in range(DC):
                        bank = (n * DC + c) % 3
                        pe.wait_ge(unit_free[bank], T.next(unit_free[bank]))
                        for t in range(GT):
                            last = turn(ps[:, bank, t * P:(t + 1) * P], xb[n][:, t, c, :])
                        last.then_inc(unit_ready[bank], 1)

            def project(slot, h, normed=None, hold=False, width=P):
                pe.wait_ge(panel_split, T.next(panel_split))
                for n in range(GROUPS):
                    if normed is not None:
                        pe.wait_ge(n_lo, normed + n + 1)
                    pe.wait_ge(unit_free[n], T.next(unit_free[n]))
                    for c in range(DC):
                        for w, x in ((w_hi, 0), (w_hi, 1), (w_lo, 0)):
                            last = M.matmul(ps[0:width, n, 0:GN], w[:, slot, c, 0:width], h(x, c, n),
                                            start=(c == 0 and x == 0 and w is w_hi), stop=(c == DC - 1 and w is w_lo))
                            if n == 0 and c == 0 and w is w_hi and x == 0 and not hold:
                                last.then_inc(panel_used, owed[0])
                                owed[0] = 0
                    last.then_inc(unit_ready[n], 1)
                owed[0] += 1

            def from_acts(h):
                return lambda x, c, n: h[x][:, 3 * n:3 * n + 3, c, :]

            per3 = [(unit_free[b], 3) for b in range(3)]
            with T.loop(pe, CC, per3 + [(panel_split, 3)]):
                for s in range(3):
                    project(s, from_acts(h_ac), normed=0)
            for s in (0, 1, 2, 0, 1, 2):
                project(s, from_acts(h_ac))
            for n in range(GROUPS):
                pe.wait_ge(unit_free[n], T.next(unit_free[n]))
                for t in range(GT):
                    last = turn(ps[:, n, t * P:(t + 1) * P], v_t[:, (3 * n + t) * P:(3 * n + t + 1) * P])
                last.then_inc(unit_ready[n], 1)
            pe.wait_ge(unit_free[0], T.next(unit_free[0]))
            pe.wait_ge(att_in, 96)
            for t in range(2):
                turn(ps[:, 0, t * P:(t + 1) * P], kc_n[:, t, :])
            turn(ps[:, 0, 2 * P:3 * P], k_t[:, 0:P]).then_inc(unit_ready[0], 1)
            r = 0
            for t in [k_t[:]] + [q_t[:, j, :] for j in range(4)]:
                for half in range(2):
                    b = r % 4
                    pe.wait_ge(acc_free[b], T.next(acc_free[b]))
                    M.matmul(ps[:, 3 + b, :], rot[:], t[:, P + 512 * half:P + 512 * (half + 1)],
                             start=True, stop=True).then_inc(acc_ready[b], 1)
                    r += 1

            for b in range(3):
                pe.wait_ge(unit_free[b], T.last(unit_free[b]) + 1)
            pe.wait_ge(rope_done, 10)
            steps = attention_steps()
            wide = [i for i, st_ in enumerate(steps) if len(st_[3]) > 3]
            for it in range(len(steps) + 3):
                if it < len(steps):
                    b, j, u, tiles = steps[it]
                    if it >= 2:
                        pe.wait_ge(s_exp, it - 1)
                    s = s_bank(it)
                    rows = slice(HD * u, HD * (u + 1))
                    q = q_t[rows, j, b * P:(b + 1) * P]
                    if b == 0:
                        runs = [(0, k_t[rows, 0:P])]
                    else:
                        own_t = [t for what, t in tiles if what == "own"]
                        runs = [(0, kc_t[rows, :]), (2 * P, k_t[rows, own_t[0] * P:(own_t[0] + 2) * P])]
                        if len(own_t) == 3:
                            runs.append((4 * P, k_t[rows, own_t[2] * P:(own_t[2] + 1) * P]))
                    for c0, keys in runs:
                        last = M.matmul(s[:, c0:c0 + keys.shape[1]], q, keys, start=True, stop=True)
                    last.then_inc(s_ready, 1)
                if 2 <= it < len(steps) + 2:
                    b, j, u, tiles = steps[it - 2]
                    pe.wait_ge(s_norm, it - 1)
                    if it >= 3:
                        pe.wait_ge(pt_a, it - 2)
                        n_wide = sum(1 for w in wide if w < it - 2)
                        if n_wide:
                            pe.wait_ge(pt_v, n_wide)
                    if it >= 7 and it % 4 == 3:
                        pe.wait_ge(mod_added, (it - 7) // 4 + 1)
                    if it >= 6 and it % 4 == 2:
                        mod_turn((it - 6) // 4)
                    for pos in range(len(tiles)):
                        bank, col = (0, pos) if pos < 3 else (1, pos - 3)
                        last = turn(ps[:, bank, col * P:(col + 1) * P], prob[(it - 2) % 3][:, pos * P:(pos + 1) * P])
                    last.then_inc(pt_ready, 1)
                if it >= 3:
                    b, j, u, tiles = steps[it - 3]
                    pe.wait_ge(pt_a, it - 2)
                    n_wide = sum(1 for w in wide if w <= it - 3)
                    if n_wide:
                        pe.wait_ge(pt_v, n_wide)
                    pair = (it - 3) // 2
                    if u == 0 and pair >= 1:
                        pe.wait_ge(ao_lo, pair)
                    cols = slice(HD * u, HD * (u + 1))
                    for pos, (what, tile) in enumerate(tiles):
                        v = v_c[:, tile, cols] if what == "ctx" else v_n[:, tile, cols]
                        last = M.matmul(ps[cols, O_BANK, 0:P], v, prT[(it - 3) % 2][:, pos, :],
                                        start=(pos == 0), stop=(pos == len(tiles) - 1))
                    last.then_inc(pv_ready, 1)
                if it:
                    late_mod(it - 1)
            mod_turn(LATE // 4 - 3)
            for k in range(len(steps) + 2, LATE):
                late_mod(k)
            mod_turn(LATE // 4 - 2)
            mod_turn(LATE // 4 - 1)

            pe.wait_ge(ao_lo, len(steps) // 2)
            pe.wait_ge(conv_m, 3 + 3 * CC)
            pe.wait_ge(mod_added, LATE // 4)

            def mixed(x, c, n):
                if c < CC:
                    return (conv_hi, conv_lo)[x][:, 3 * n:3 * n + 3, c, :]
                return (at_hi, at_lo)[x][:, 3 * n:3 * n + 3, c - CC, :]

            def out_project(s0, h):
                with T.loop(pe, 2, [(unit_free[b], 4) for b in range(3)] + [(panel_split, 4)]):
                    for s in range(4):
                        project((s0 + s) % SLOTS, h)

            out_project(0, mixed)
            pe.wait_ge(mods_ready, 2)
            both_norms(sq_a, sq_c)

            def down(p, slots):
                pe.wait_ge(panel_split, T.next(panel_split))
                for n in range(GROUPS):
                    pe.wait_ge(hid_lo, T.next(hid_lo, 4 if n == 0 else 1))
                    for c in range(DC):
                        b = c % 4
                        pe.wait_ge(acc_free[b], T.next(acc_free[b]))
                        for f in range(2):
                            if f == 1 and n == 0 and c == 0:
                                pe.wait_ge(panel_split, T.next(panel_split))
                            for w, x in ((w_hi, 0), (w_hi, 1), (w_lo, 0)):
                                first = f == 0 and w is w_hi and x == 0
                                last = M.matmul(ps[:, 3 + b, 0:GN], w[:, slots[f], c, :],
                                                hidden[p][x][:, f, GN * n:GN * (n + 1)],
                                                start=first, stop=(f == 1 and w is w_lo))
                                if first and n == 0 and c == 0:
                                    last.then_inc(panel_used, owed[0])
                                    owed[0] = 0
                        last.then_inc(acc_ready[b], 1)
                owed[0] += 2

            def mlp(h, s0, normed):
                a = [(s0 + s) % SLOTS for s in (0, 1)]
                b = [(s0 + s) % SLOTS for s in (2, 3)]
                project(a[0], from_acts(h), normed=normed)
                project(a[1], from_acts(h), hold=True)
                per = [(unit_free[n], 4) for n in range(3)] + [(acc_free[n], 12) for n in range(4)]
                with T.loop(pe, (PAIRS - 2) // 2, per + [(panel_split, 8), (hid_lo, 12)]):
                    for p in range(2):
                        project(b[0], from_acts(h))
                        project(b[1], from_acts(h))
                        down(p, a)
                project(b[0], from_acts(h))
                project(b[1], from_acts(h))
                down(0, a)
                down(1, b)

            mlp(h_ac, 0, 3)
            if STAGE < 2:
                both_norms(sq_a, None, final=True)
                return
            both_norms(sq_a, sq_c)
            project(0, from_acts(h_ac), normed=6, width=2 * RANK)
            for part in range(2):
                for s in range(4):
                    project((1 + s) % SLOTS, from_acts(h_ac))
            with T.loop(pe, 2, [(unit_free[b], 4) for b in range(3)] + [(panel_split, 4)] + [(acc_free[b], 3) for b in range(4)]):
                for s in range(4):
                    slot = (1 + s) % SLOTS
                    pe.wait_ge(panel_split, T.next(panel_split))
                    for n in range(GROUPS):
                        pe.wait_ge(unit_free[n], T.next(unit_free[n]))
                        for c in range(DC):
                            for w, x in ((w_hi, 0), (w_hi, 1), (w_lo, 0)):
                                first = c == 0 and w is w_hi and x == 0
                                last = M.matmul(ps[:, n, 0:GN], w[:, slot, c, :], h_ac[x][:, 3 * n:3 * n + 3, c, :],
                                                start=first, stop=(c == DC - 1 and w is w_lo))
                                if first and n == 0:
                                    last.then_inc(panel_used, 1)
                        last.then_inc(unit_ready[n], 1)
                        u = 3 * s + n
                        if u:
                            m = (u - 1) % 3
                            pe.wait_ge(unit_free[m], T.last(unit_free[m]) + 1)
                            b = (u - 1) % 4
                            pe.wait_ge(acc_free[b], T.next(acc_free[b]))
                            for t in range(GT):
                                last = turn(ps[:, 3 + b, t * P:(t + 1) * P], v_tmp[(u - 1) % 2][:, t * P:(t + 1) * P])
                            last.then_inc(acc_ready[b], 1)
                pe.wait_ge(unit_free[2], T.last(unit_free[2]) + 1)
                pe.wait_ge(acc_free[3], T.next(acc_free[3]))
                for t in range(GT):
                    last = turn(ps[:, 6, t * P:(t + 1) * P], v_tmp[1][:, t * P:(t + 1) * P])
                last.then_inc(acc_ready[3], 1)
            out_project(1, from_acts(h_ac))

            pe.wait_ge(gla_in, 32)
            for d in range(2):
                for h in range(GH):
                    for n in range(GROUPS):
                        pe.wait_ge(unit_free[n], T.next(unit_free[n]))
                        M.matmul(ps[:, n, 0:GN], gw[:, d, h * P:(h + 1) * P], r_t[:, GN * n:GN * (n + 1)],
                                 start=True, stop=True).then_inc(unit_ready[n], 1)
            for n in range(3):
                pe.wait_ge(unit_free[n], T.last(unit_free[n]) + 1)
            for b in range(4):
                pe.wait_ge(acc_free[b], T.last(acc_free[b]) + 1)

            order = terms()
            count = {"k": 0, "pair": 0}

            def turn_k(i):
                pe.wait_ge(xt_ready, i + 1)
                count["k"] += 1
                if count["k"] > 1:
                    pe.wait_ge(khn_ready, count["k"] - 1)
                for h in range(GH):
                    last = turn(ps[:, 2, h * P:(h + 1) * P], kh[:, h, :])
                last.then_inc(khn_t, 1)

            def update(tile):
                pe.wait_ge(khn_ready, count["k"])
                if count["k"] > 1:
                    pe.wait_ge(st_ready, count["k"] - 1)
                for h in range(GH):
                    last = M.matmul(psf[:, 5 * 512 + DV * h:5 * 512 + DV * (h + 1)], khn[:, h, :],
                                    gv[:, tile, DV * h:DV * (h + 1)], start=True, stop=True)
                last.then_inc(upd_ready, 1)

            i = 0
            n_ob = 0
            for tile in [0] + list(range(TILES - 1, 0, -1)):
                if tile != 1:
                    turn_k(i)
                    i += 1
                if tile:
                    pe.wait_ge(xt_ready, i + 1)
                    i += 1
                    if n_ob:
                        pe.wait_ge(ob_taken, n_ob)
                        pe.wait_ge(st_ready, 1 + n_ob)
                    else:
                        pe.wait_ge(st_in, 16)
                    for h in range(GH):
                        last = M.matmul(psf[:, 3 * 512 + DV * h:3 * 512 + DV * (h + 1)], qh[:, h, :], st[:, h, :],
                                        start=True, stop=True)
                    last.then_inc(ob_ready, 1)
                    n_ob += 1
                if tile != 1:
                    update(tile)

            def grams(item, stationary, moving):
                if item >= 2:
                    prev = item - 2
                    if prev % 15 == 0:
                        pe.wait_ge(diag_ready, prev // 15 + 1)
                    else:
                        pe.wait_ge(gram_taken, 14 * (prev // 15) + prev % 15)
                for h in range(GH):
                    last = M.matmul(ps[:, item % 2, h * P:(h + 1) * P], stationary[:, h, :], moving[:, h, :],
                                    start=True, stop=True)
                last.then_inc(gram_ready, 1)

            def turn_o(tile, half):
                if half == 0:
                    pe.wait_ge(o_nrm, tile + 1)
                if tile or half:
                    pe.wait_ge(ot_taken, 2 * tile + half)
                for c in range(4):
                    last = turn(ps[:, 7, c * P:(c + 1) * P], oo[:, (4 * half + c) * P:(4 * half + c + 1) * P])
                last.then_inc(ot_ready, 1)

            for tile in range(TILES):
                grams(15 * tile, gk[:, tile], gq[:, tile])
                for jj in range(14):
                    pe.wait_ge(xt_ready, i + 1)
                    i += 1
                    x = xx[jj % 2]
                    grams(15 * tile + 1 + jj, x, x)
                    if tile and jj == 3:
                        turn_o(tile - 1, 0)
                    if tile and jj == 5:
                        turn_o(tile - 1, 1)
                if tile:
                    pe.wait_ge(xt_ready, i + 1)
                    i += 1
                if tile < TILES - 1:
                    turn_k(i)
                    i += 1
                pe.wait_ge(gram_taken, 14 * (tile + 1))
                pe.wait_ge(ob_taken, TILES - 1)
                if tile:
                    pe.wait_ge(o_sum, tile)
                    pe.wait_ge(st_ready, 8 + tile)
                    pe.wait_ge(st_in, 32)
                for h in range(GH):
                    o = psf[:, 3 * 512 + DV * h:3 * 512 + DV * (h + 1)]
                    last = M.matmul(o, att[tile % 2][:, h, :], gv[:, tile, DV * h:DV * (h + 1)], start=True, stop=(tile == 0))
                    if tile:
                        last = M.matmul(o, qh[:, h, :], st[:, h, :], start=False, stop=True)
                last.then_inc(o_ready, 1)
                if tile < TILES - 1:
                    update(tile)
            for half in range(2):
                turn_o(TILES - 1, half)

            pe.wait_ge(gm_lo, TILES)
            out_project(1, lambda x, c, n: (m_hi, m_lo)[x][:, 3 * n:3 * n + 3, c, :])
            both_norms(sq_b, sq_c)
            mlp(h_bc, 1, 9)
            both_norms(sq_b, None, final=True)


def tables():
    f32 = np.float32
    quarter = HD // 4
    inv = (f32(10000.0) ** (-(np.arange(quarter, dtype=f32) * f32(2.0) / f32(2 * quarter)))).astype(f32)
    pos = np.arange(LAT)
    f = np.arange(P) % HD
    where = np.where((f < HD // 2)[:, None], (pos // 64)[None, :], (pos % 64)[None, :]).astype(f32)
    ang = (where * inv[f % quarter][:, None]).astype(f32)
    rot = np.zeros((P, P), f32)
    for m in range(P):
        if m % (2 * quarter) < quarter:
            rot[m + quarter, m] = -1.0
        else:
            rot[m - quarter, m] = 1.0
    q, key = np.arange(P)[:, None], np.arange(P)[None, :]
    band = np.stack([np.where(key >= q, 0.0, -BAND), np.where(key <= q, 0.0, -BAND)], 1).astype(f32)
    masks = np.zeros((P, 2 * len(LEVELS), P), f32)
    for i, n in enumerate(LEVELS):
        same = (q // (2 * n)) == (key // (2 * n))
        masks[:, 2 * i] = same & (q // n % 2 == 0) & (key // n % 2 == 1)
        masks[:, 2 * i + 1] = same & (q // n % 2 == 1) & (key // n % 2 == 0)
    return {"c_ident": np.eye(P, dtype=f32), "c_cos": np.cos(ang).astype(f32), "c_sin": np.sin(ang).astype(f32),
            "c_rot": rot, "c_band": band, "c_masks": masks}


_INS = ["x_prompt", "x_sample", "cache_k", "cache_v", "state_fwd", "state_bwd", "c", "c_ctx", "mod_w", "mod_b", "norm_g",
        "ab_w_in", "conv_w", "attn_sink", "ab_w_out", "gla_w_in", "gla_gate_w", "gla_gate_b", "gla_norm_g", "gla_w_out",
        "mlp_w1", "mlp_w2"]
_OUTS = [("y_prompt", (1, P, D)), ("y_sample", (1, LAT, D)), ("new_cache_k", (1, 1, P, 2, HD)),
         ("new_cache_v", (1, 1, P, 2, HD)), ("new_state_fwd", (1, 1, GH, P, DV)), ("new_state_bwd", (1, 1, GH, P, DV))]


def kernel(**inputs):
    import concourse.bacc as bacc
    from concourse.bass_utils import run_bass_kernel_spmd

    nc = bacc.Bacc("TRN2", target_bir_lowering=False, num_devices=1)
    arrays = {name: np.ascontiguousarray(inputs[name]) for name in _INS}
    arrays.update(tables())
    io = {name: nc.dram_tensor(name, a.shape, mybir.dt.from_np(a.dtype), kind="ExternalInput").ap()
          for name, a in arrays.items()}
    for name, shape in _OUTS:
        io[name] = nc.dram_tensor(name, shape, F32, kind="ExternalOutput").ap()
    for name in ("x_scratch", "og_scratch"):
        io[name] = nc.dram_tensor(name, (TILES, P, D), F32, kind="Internal").ap()
    build(nc, io)
    got = run_bass_kernel_spmd(nc, [arrays], core_ids=[0]).results[0]
    return tuple(got[name] for name, _ in _OUTS)
```
